# Optimizing a Trainium2 kernel written in Bass

```python
import math
import jax, jax.numpy as jnp
from jax import lax
import numpy as np

D_MODEL = 1024
BATCH = 1
SEQ = 512
DEPTH = 2

CHUNK = 64
Q_BLOCK = 128
N_MIXERS = 2
FOX_HEADS = 16
FOX_HEAD_DIM = D_MODEL // FOX_HEADS
HGRN_EXPAND = 128
HGRN_HEADS = D_MODEL // HGRN_EXPAND
HGRN_HEAD_DIM = HGRN_EXPAND
D_FF = -(-8 * D_MODEL // (3 * 256)) * 256
N_FOX = (DEPTH + 1) // 2
N_HGRN = DEPTH // 2
EPS = 1e-6


def rmsnorm(x, g):
    x32 = x.astype(jnp.float32)
    y = x32 * lax.rsqrt(jnp.mean(x32 * x32, axis=-1, keepdims=True) + EPS)
    return (y * g.astype(jnp.float32)).astype(x.dtype)

def fox_attention(h, w_in, b_f, w_out):
    bsz, seq, _ = h.shape
    proj = jnp.einsum('bsd,de->bse', h, w_in)
    q, k, v, f_logit = jnp.split(proj, [D_MODEL, 2 * D_MODEL, 3 * D_MODEL], axis=-1)

    def heads(t):
        return t.reshape(bsz, seq, FOX_HEADS, FOX_HEAD_DIM).transpose(0, 2, 1, 3)

    q = heads(q) * (FOX_HEAD_DIM ** -0.5)
    k = heads(k)
    v = heads(v)
    log_f = jax.nn.log_sigmoid(f_logit.astype(jnp.float32) + b_f.astype(jnp.float32))
    c = jnp.cumsum(log_f, axis=1).transpose(0, 2, 1)
    key_pos = jnp.arange(seq)

    def q_block(blk):
        start = blk * Q_BLOCK
        qb = lax.dynamic_slice_in_dim(q, start, Q_BLOCK, axis=2)
        cb = lax.dynamic_slice_in_dim(c, start, Q_BLOCK, axis=2)
        q_pos = start + jnp.arange(Q_BLOCK)
        logits = jnp.einsum('bhqd,bhkd->bhqk', qb, k).astype(jnp.float32)
        logits = logits + cb[:, :, :, None] - c[:, :, None, :]
        logits = jnp.where(q_pos[:, None] >= key_pos[None, :], logits, -jnp.inf)
        p = jax.nn.softmax(logits, axis=-1).astype(v.dtype)
        return jnp.einsum('bhqk,bhkd->bhqd', p, v)

    out = lax.map(q_block, jnp.arange(seq // Q_BLOCK))
    out = out.transpose(1, 0, 3, 2, 4).reshape(bsz, seq, D_MODEL)
    return jnp.einsum('bsd,de->bse', out, w_out)

def hgrn2_recurrence(h, w_in, lb, g_norm_w, w_out):
    bsz, seq, _ = h.shape
    n_chunks = seq // CHUNK
    proj = jnp.einsum('bsd,de->bse', h, w_in)
    q, f_logit, i_val, g = jnp.split(proj, [D_MODEL, 2 * D_MODEL, 3 * D_MODEL], axis=-1)
    f = lb + (1.0 - lb) * jax.nn.sigmoid(f_logit.astype(jnp.float32))
    log_f = jnp.log(f)
    k = 1.0 - f

    def to_chunks(t):
        t = t.astype(jnp.float32).reshape(bsz, n_chunks, CHUNK, HGRN_HEADS, HGRN_HEAD_DIM)
        return t.transpose(1, 0, 3, 2, 4)

    qc = to_chunks(q)
    kc = to_chunks(k)
    vc = to_chunks(i_val)
    bc = jnp.cumsum(to_chunks(log_f), axis=3)
    causal = jnp.arange(CHUNK)[:, None] >= jnp.arange(CHUNK)[None, :]

    def step(state, xs):
        q_t, k_t, v_t, b_t = xs
        o_inter = jnp.einsum('bhtk,bhkv->bhtv', q_t * jnp.exp(b_t), state)
        diff = b_t[:, :, :, None, :] - b_t[:, :, None, :, :]
        decay = jnp.exp(jnp.where(causal[:, :, None], diff, -jnp.inf))
        scores = jnp.einsum('bhtk,bhsk,bhtsk->bhts', q_t, k_t, decay)
        o = o_inter + jnp.einsum('bhts,bhsv->bhtv', scores, v_t)
        b_last = b_t[:, :, -1, :]
        k_dec = k_t * jnp.exp(b_last[:, :, None, :] - b_t)
        new_state = jnp.exp(b_last)[..., None] * state + jnp.einsum('bhsk,bhsv->bhkv', k_dec, v_t)
        return new_state, o

    state0 = jnp.zeros((bsz, HGRN_HEADS, HGRN_HEAD_DIM, HGRN_HEAD_DIM), jnp.float32)
    _, o = lax.scan(step, state0, (qc, kc, vc, bc))
    o = o.transpose(1, 0, 3, 2, 4).reshape(bsz, seq, HGRN_HEADS, HGRN_HEAD_DIM)
    g = g.astype(jnp.float32).reshape(bsz, seq, HGRN_HEADS, HGRN_HEAD_DIM)
    o = rmsnorm(o, g_norm_w) * jax.nn.silu(g)
    return jnp.einsum('bsd,de->bse', o.reshape(bsz, seq, D_MODEL).astype(h.dtype), w_out)

def swiglu_ffn(h, w_in, w_out):
    gate, up = jnp.split(jnp.einsum('bsd,df->bsf', h, w_in), 2, axis=-1)
    return jnp.einsum('bsf,fd->bsd', jax.nn.silu(gate) * up, w_out)

def first_inputs(seed: int = 0) -> dict:
    key = jax.random.key(seed)
    ks = jax.random.split(key, 11)
    f32 = jnp.float32

    def normal(k, shape, fan_in):
        return jax.random.normal(k, shape, f32) * (fan_in ** -0.5)

    x = jax.random.normal(ks[0], (BATCH, SEQ, D_MODEL), f32)
    fox_w_in = normal(ks[1], (N_FOX, D_MODEL, 3 * D_MODEL + FOX_HEADS), D_MODEL)
    fox_b_f = jax.random.uniform(ks[2], (N_FOX, FOX_HEADS), f32, 1.0, 4.0)
    fox_w_out = normal(ks[3], (N_FOX, D_MODEL, D_MODEL), D_MODEL)
    hgrn_w_in = normal(ks[4], (N_HGRN, D_MODEL, 4 * D_MODEL), D_MODEL)
    hgrn_lb_table = 0.5 * jax.random.normal(ks[5], (DEPTH + 1, D_MODEL), f32)
    hgrn_gnorm = 1.0 + 0.02 * jax.random.normal(ks[6], (N_HGRN, HGRN_HEAD_DIM), f32)
    hgrn_w_out = normal(ks[7], (N_HGRN, D_MODEL, D_MODEL), D_MODEL)
    ffn_w_in = normal(ks[8], (DEPTH, D_MODEL, 2 * D_FF), D_MODEL)
    ffn_w_out = normal(ks[9], (DEPTH, D_FF, D_MODEL), D_FF)
    norm_gains = 1.0 + 0.02 * jax.random.normal(ks[10], (DEPTH, 4, D_MODEL), f32)
    return {'x': x, 'fox_w_in': fox_w_in, 'fox_b_f': fox_b_f, 'fox_w_out': fox_w_out,
            'hgrn_w_in': hgrn_w_in, 'hgrn_lb_table': hgrn_lb_table, 'hgrn_gnorm': hgrn_gnorm,
            'hgrn_w_out': hgrn_w_out, 'ffn_w_in': ffn_w_in, 'ffn_w_out': ffn_w_out,
            'norm_gains': norm_gains}

def first_block(x, fox_w_in, fox_b_f, fox_w_out, hgrn_w_in, hgrn_lb_table, hgrn_gnorm,
              hgrn_w_out, ffn_w_in, ffn_w_out, norm_gains):
    lower_bounds = jnp.cumsum(jax.nn.softmax(hgrn_lb_table.astype(jnp.float32), axis=0), axis=0)
    h = x
    for layer in range(DEPTH):
        j = layer // N_MIXERS
        hn = rmsnorm(h, norm_gains[layer, 0])
        if layer % N_MIXERS == 0:
            mixed = fox_attention(hn, fox_w_in[j], fox_b_f[j], fox_w_out[j])
        else:
            mixed = hgrn2_recurrence(hn, hgrn_w_in[j], lower_bounds[layer], hgrn_gnorm[j],
                                     hgrn_w_out[j])
        h = h + rmsnorm(mixed, norm_gains[layer, 1])
        hn = rmsnorm(h, norm_gains[layer, 2])
        h = h + rmsnorm(swiglu_ffn(hn, ffn_w_in[layer], ffn_w_out[layer]), norm_gains[layer, 3])
    return h


NORM_EPS = 1e-6

SB_HEADS = 8
SB_HEAD_DIM = 64
SB_WIDTH = SB_HEADS * SB_HEAD_DIM
POOL_WINDOWS = (2, 4, 8, 16)
POOL_GROUPS = len(POOL_WINDOWS)
POOL_WIDTH = D_MODEL - SB_WIDTH
POOL_GROUP_DIM = POOL_WIDTH // POOL_GROUPS
EVEN_IN_WIDTH = 3 * SB_WIDTH + POOL_WIDTH
EVEN_MIX_WIDTH = SB_WIDTH + POOL_WIDTH

GLA_HEADS = 4
GLA_KEY_WIDTH = D_MODEL // 2
GLA_VALUE_WIDTH = D_MODEL
GLA_KEY_DIM = GLA_KEY_WIDTH // GLA_HEADS
GLA_VALUE_DIM = GLA_VALUE_WIDTH // GLA_HEADS
GLA_GATE_RANK = 16
GLA_TAU = 16.0
ODD_IN_WIDTH = 2 * GLA_KEY_WIDTH + 2 * GLA_VALUE_WIDTH + GLA_GATE_RANK

FFN_HIDDEN = 2816
CONV_WIDTH = 3

N_EVEN = (DEPTH + 1) // 2
N_ODD = DEPTH // 2


def rms_norm(x, gain):
    xf = x.astype(jnp.float32)
    y = xf * lax.rsqrt(jnp.mean(xf * xf, axis=-1, keepdims=True) + NORM_EPS)
    return (y * gain.astype(jnp.float32)).astype(x.dtype)

def stick_breaking_attention(q, k, v):
    b, s, h, dh = q.shape
    qh = jnp.transpose(q, (0, 2, 1, 3))
    kh = jnp.transpose(k, (0, 2, 1, 3))
    vh = jnp.transpose(v, (0, 2, 1, 3))
    scale = dh ** -0.5
    key_pos = jnp.arange(s)

    def block(i):
        start = i * Q_BLOCK
        q_blk = lax.dynamic_slice_in_dim(qh, start, Q_BLOCK, axis=2)
        z = jnp.einsum('bhqd,bhkd->bhqk', q_blk, kh,
                       preferred_element_type=jnp.float32) * scale
        q_pos = start + jnp.arange(Q_BLOCK)
        visible = key_pos[None, :] < q_pos[:, None]
        log_fail = jnp.where(visible, jax.nn.log_sigmoid(-z), 0.0)
        cum_rev = lax.cumsum(log_fail, axis=3, reverse=True)
        later = jnp.concatenate([cum_rev[..., 1:], jnp.zeros_like(cum_rev[..., :1])], axis=-1)
        weights = jnp.where(visible, jnp.exp(jax.nn.log_sigmoid(z) + later), 0.0)
        return jnp.einsum('bhqk,bhkd->bhqd', weights.astype(vh.dtype), vh)

    out = lax.map(block, jnp.arange(s // Q_BLOCK))
    return jnp.transpose(out, (1, 0, 3, 2, 4)).reshape(b, s, h * dh)

def multiscale_pool(xb, pool_w, pool_scale):
    b, s, _ = xb.shape
    groups = xb.reshape(b, s, POOL_GROUPS, POOL_GROUP_DIM)
    prefix = jnp.cumsum(groups.astype(jnp.float32), axis=1)
    prefix = jnp.pad(prefix, ((0, 0), (1, 0), (0, 0), (0, 0)))
    pos = jnp.arange(1, s + 1, dtype=jnp.float32)
    outs = []
    for g, w in enumerate(POOL_WINDOWS):
        pg = jnp.pad(prefix[:, :, g], ((0, 0), (w - 1, 0), (0, 0)))
        window_sum = pg[:, w:] - pg[:, :s]
        count = jnp.minimum(pos, float(w))[None, :, None]
        pooled = window_sum / count - groups[:, :, g].astype(jnp.float32)
        outs.append(jnp.einsum('bsc,cd->bsd', pooled.astype(xb.dtype), pool_w[g]))
    return jnp.concatenate(outs, axis=-1) * pool_scale

def gated_linear_attention(q, k, v, log_alpha):
    b, s, h, dk = q.shape
    dv = v.shape[-1]
    n = s // CHUNK

    def chunks(t):
        return jnp.moveaxis(t.reshape(b, n, CHUNK, h, t.shape[-1]), 1, 0)

    qc = chunks(q.astype(jnp.float32))
    kc = chunks(k.astype(jnp.float32))
    vc = chunks(v.astype(jnp.float32))
    cum = jnp.cumsum(chunks(log_alpha), axis=2)
    total = cum[:, :, -1]
    k_dec = kc * jnp.exp(total[:, :, None] - cum)
    chunk_decay = jnp.exp(total)

    def step(state, inp):
        q_c, k_c, v_c, decay_c = inp
        state = decay_c[..., None] * state + jnp.einsum('bchk,bchv->bhkv', k_c, v_c)
        return state, jnp.einsum('bchk,bhkv->bchv', q_c, state)

    state0 = jnp.zeros((b, h, dk, dv), jnp.float32)
    _, out = lax.scan(step, state0, (qc, k_dec, vc, chunk_decay))
    return jnp.moveaxis(out, 0, 1).reshape(b, s, h, dv)

def even_mixer(h, w_in, q_gain, k_gain, pool_w, pool_scale, w_out):
    b, s, _ = h.shape
    proj = h @ w_in
    q, k, v, xb = jnp.split(proj, [SB_WIDTH, 2 * SB_WIDTH, 3 * SB_WIDTH], axis=-1)
    q = rms_norm(q.reshape(b, s, SB_HEADS, SB_HEAD_DIM), q_gain)
    k = rms_norm(k.reshape(b, s, SB_HEADS, SB_HEAD_DIM), k_gain)
    v = v.reshape(b, s, SB_HEADS, SB_HEAD_DIM)
    o_a = stick_breaking_attention(q, k, v)
    o_b = multiscale_pool(xb, pool_w, pool_scale)
    return jnp.concatenate([o_a.astype(h.dtype), o_b.astype(h.dtype)], axis=-1) @ w_out

def odd_mixer(h, w_in, w_a2, b_a, o_gain, w_out):
    b, s, _ = h.shape
    proj = h @ w_in
    q, k, v, r, a_low = jnp.split(
        proj, [GLA_KEY_WIDTH, 2 * GLA_KEY_WIDTH, 2 * GLA_KEY_WIDTH + GLA_VALUE_WIDTH,
               2 * GLA_KEY_WIDTH + 2 * GLA_VALUE_WIDTH], axis=-1)
    q = q.reshape(b, s, GLA_HEADS, GLA_KEY_DIM) * (GLA_KEY_DIM ** -0.5)
    k = k.reshape(b, s, GLA_HEADS, GLA_KEY_DIM)
    v = v.reshape(b, s, GLA_HEADS, GLA_VALUE_DIM)
    gate_logit = (a_low @ w_a2 + b_a).astype(jnp.float32).reshape(b, s, GLA_HEADS, GLA_KEY_DIM)
    log_alpha = jax.nn.log_sigmoid(gate_logit) / GLA_TAU
    o = gated_linear_attention(q, k, v, log_alpha)
    o = rms_norm(o, o_gain).reshape(b, s, GLA_VALUE_WIDTH).astype(h.dtype)
    return (o * jax.nn.silu(r)) @ w_out

def conv_ffn(h, w_up, conv_w, conv_b, w_down):
    s = h.shape[1]
    u = h @ w_up
    up = jnp.pad(u, ((0, 0), (CONV_WIDTH - 1, 0), (0, 0)))
    conv = conv_b
    for j in range(CONV_WIDTH):
        conv = conv + conv_w[j] * up[:, j:j + s]
    a, g = jnp.split(conv, 2, axis=-1)
    return (jax.nn.silu(a) * g) @ w_down

def second_inputs(seed: int = 0) -> dict:
    key = jax.random.key(seed)
    ks = jax.random.split(key, 20)
    f32 = jnp.float32

    def nrm(k, shape, scale):
        return jax.random.normal(k, shape, f32) * scale

    return {
        "x": nrm(ks[0], (BATCH, SEQ, D_MODEL), 1.0),
        "mix_norm_even": 1.0 + nrm(ks[1], (N_EVEN, D_MODEL), 0.02),
        "w_in_even": nrm(ks[2], (N_EVEN, D_MODEL, EVEN_IN_WIDTH), D_MODEL ** -0.5),
        "sb_q_gain": 1.0 + nrm(ks[3], (N_EVEN, SB_HEAD_DIM), 0.02),
        "sb_k_gain": 1.0 + nrm(ks[4], (N_EVEN, SB_HEAD_DIM), 0.02),
        "pool_w": nrm(ks[5], (N_EVEN, POOL_GROUPS, POOL_GROUP_DIM, POOL_GROUP_DIM), POOL_GROUP_DIM ** -0.5),
        "pool_scale": 1.0 + nrm(ks[6], (N_EVEN, POOL_WIDTH), 0.1),
        "w_out_even": nrm(ks[7], (N_EVEN, EVEN_MIX_WIDTH, D_MODEL), EVEN_MIX_WIDTH ** -0.5),
        "mix_norm_odd": 1.0 + nrm(ks[8], (N_ODD, D_MODEL), 0.02),
        "w_in_odd": nrm(ks[9], (N_ODD, D_MODEL, ODD_IN_WIDTH), D_MODEL ** -0.5),
        "gla_w_a2": nrm(ks[10], (N_ODD, GLA_GATE_RANK, GLA_KEY_WIDTH), GLA_GATE_RANK ** -0.5),
        "gla_b_a": nrm(ks[11], (N_ODD, GLA_KEY_WIDTH), 0.01),
        "gla_o_gain": 1.0 + nrm(ks[12], (N_ODD, GLA_VALUE_DIM), 0.02),
        "w_out_odd": nrm(ks[13], (N_ODD, GLA_VALUE_WIDTH, D_MODEL), GLA_VALUE_WIDTH ** -0.5),
        "ffn_norm": 1.0 + nrm(ks[14], (DEPTH, D_MODEL), 0.02),
        "ffn_w_up": nrm(ks[15], (DEPTH, D_MODEL, 2 * FFN_HIDDEN), D_MODEL ** -0.5),
        "ffn_conv_w": nrm(ks[16], (DEPTH, CONV_WIDTH, 2 * FFN_HIDDEN), CONV_WIDTH ** -0.5),
        "ffn_conv_b": nrm(ks[17], (DEPTH, 2 * FFN_HIDDEN), 0.01),
        "ffn_w_down": nrm(ks[18], (DEPTH, FFN_HIDDEN, D_MODEL), FFN_HIDDEN ** -0.5),
    }

def second_block(x, mix_norm_even, w_in_even, sb_q_gain, sb_k_gain, pool_w, pool_scale, w_out_even,
              mix_norm_odd, w_in_odd, gla_w_a2, gla_b_a, gla_o_gain, w_out_odd,
              ffn_norm, ffn_w_up, ffn_conv_w, ffn_conv_b, ffn_w_down):
    for layer in range(DEPTH):
        if layer % 2 == 0:
            i = layer // 2
            x = x + even_mixer(rms_norm(x, mix_norm_even[i]), w_in_even[i], sb_q_gain[i],
                               sb_k_gain[i], pool_w[i], pool_scale[i], w_out_even[i])
        else:
            i = layer // 2
            x = x + odd_mixer(rms_norm(x, mix_norm_odd[i]), w_in_odd[i], gla_w_a2[i],
                              gla_b_a[i], gla_o_gain[i], w_out_odd[i])
        x = x + conv_ffn(rms_norm(x, ffn_norm[layer]), ffn_w_up[layer], ffn_conv_w[layer],
                         ffn_conv_b[layer], ffn_w_down[layer])
    return x


def setup_inputs(seed=0):
    out = dict(first_inputs(seed))
    for name, value in second_inputs(seed + 1).items():
        if name != "x":
            out[name + "_2"] = value
    return out


def reference(
    x, fox_w_in, fox_b_f, fox_w_out, hgrn_w_in, hgrn_lb_table, hgrn_gnorm, hgrn_w_out, ffn_w_in,
    ffn_w_out, norm_gains, mix_norm_even_2, w_in_even_2, sb_q_gain_2, sb_k_gain_2, pool_w_2,
    pool_scale_2, w_out_even_2, mix_norm_odd_2, w_in_odd_2, gla_w_a2_2, gla_b_a_2, gla_o_gain_2,
    w_out_odd_2, ffn_norm_2, ffn_w_up_2, ffn_conv_w_2, ffn_conv_b_2, ffn_w_down_2,
):
    x = first_block(
        x, fox_w_in, fox_b_f, fox_w_out, hgrn_w_in, hgrn_lb_table, hgrn_gnorm, hgrn_w_out,
        ffn_w_in, ffn_w_out, norm_gains,
    )
    return second_block(
        x, mix_norm_even_2, w_in_even_2, sb_q_gain_2, sb_k_gain_2, pool_w_2, pool_scale_2,
        w_out_even_2, mix_norm_odd_2, w_in_odd_2, gla_w_a2_2, gla_b_a_2, gla_o_gain_2,
        w_out_odd_2, ffn_norm_2, ffn_w_up_2, ffn_conv_w_2, ffn_conv_b_2, ffn_w_down_2,
    )


_drawn_inputs = setup_inputs


def setup_inputs(seed=0):
    import zlib

    import numpy as np

    out = dict(_drawn_inputs(seed))
    spreads = {}
    factors = {'hgrn_gnorm': 4.157,
     'mix_norm_even_2': 6.95,
     'sb_q_gain_2': 8.0,
     'sb_k_gain_2': 8.0,
     'mix_norm_odd_2': 5.328,
     'gla_b_a_2': 32.794,
     'gla_o_gain_2': 24.482,
     'ffn_norm_2': 5.411,
     'ffn_conv_b_2': 8.0}
    for name, (base, spread) in spreads.items():
        noise = np.random.default_rng([zlib.crc32(name.encode()), seed]).standard_normal(out[name].shape)
        drawn = base * np.exp(spread * noise) if base else spread * noise
        out[name] = __import__('jax').numpy.asarray(drawn.astype(out[name].dtype))
    for name, factor in factors.items():
        out[name] = (out[name] * factor).astype(out[name].dtype)
    return out
```

```python
from contextlib import ExitStack, contextmanager

import concourse.bass as bass
import numpy as np
from concourse import mybir

F32 = mybir.dt.float32
F32R = mybir.dt.float32r
U32 = mybir.dt.uint32
ACT = mybir.ActivationFunctionType
ALU = mybir.AluOpType
AX_X = mybir.AxisListType.X

P = 128
T = 512
TT = T // P
D = 1024
DT = D // P
FF = 2816
FT = FF // P
IN_UNIT = DT * P
DOWN_BLOCKS = FT // 2
DOWN_UNIT = DOWN_BLOCKS * P
RAW_SLOTS, SPLIT_SLOTS = 2, 4
EPS = 1e-6
CHUNK = 64
NCH = T // CHUNK
FOX_PAIRS, FOX_HEADS = 8, 16
LOG_F_MIN = -17.0
NEG = -1e30
SB_DIM = 64
GLA_TAU = 16.0



def repeat(eng, lo, hi, body):
    if hi - lo == 1:
        body(lo)
    elif hi > lo:
        with eng.Fori(lo, hi, 1) as j:
            body(j)


class Phase:

    def __init__(self, name, first, count, size):
        self.name, self.first, self.count, self.size = name, first, count, size


def plan_phases():
    ph, at = {}, 0
    for name, count, size in (
        ("fox_v", 8, IN_UNIT), ("fox_qk", 16, IN_UNIT), ("fox_out", 8, IN_UNIT),
        ("up0", 2 * FT, IN_UNIT), ("down0", 2 * DT, DOWN_UNIT),
        ("hgrn_v", 8, IN_UNIT), ("hgrn_g", 8, IN_UNIT), ("hgrn_qf", 16, IN_UNIT), ("hgrn_out", 8, IN_UNIT),
        ("up1", 2 * FT, IN_UNIT), ("down1", 2 * DT, DOWN_UNIT),
        ("sb_v", 4, IN_UNIT), ("sb_x", 4, IN_UNIT), ("sb_qk", 8, IN_UNIT), ("sb_out", 8, IN_UNIT),
        ("up2", 2 * FT, IN_UNIT), ("down2", 2 * DT, DOWN_UNIT),
        ("gla_v", 8, IN_UNIT), ("gla_r", 8, IN_UNIT), ("gla_qk", 8, IN_UNIT), ("gla_out", 8, IN_UNIT),
        ("up3", 2 * FT, IN_UNIT), ("down3", 2 * DT, DOWN_UNIT),
    ):
        ph[name] = Phase(name, at, count, size)
        at += count
    return ph, at


COL, _at = {}, 0
for _name, _n in (
    ("gain", 8 * DT), ("mix_even", DT), ("ffn_norm0", DT), ("mix_odd", DT), ("ffn_norm1", DT),
    ("fox_b", 1), ("lb_table", 3 * DT), ("hgrn_norm", 1), ("sb_q", 1), ("sb_k", 1), ("pool_scale", 4),
    ("gla_b", 4), ("gla_norm", 2), ("onehot", FOX_HEADS), ("conv0", 4 * 2 * FT), ("conv1", 4 * 2 * FT),
):
    COL[_name] = _at
    _at += _n
N_COLS = _at
PRE_GAIN = [COL["gain"], COL["gain"] + 2 * DT, COL["gain"] + 4 * DT, COL["gain"] + 6 * DT,
            COL["mix_even"], COL["ffn_norm0"], COL["mix_odd"], COL["ffn_norm1"]]
POST_GAIN = [COL["gain"] + DT, COL["gain"] + 3 * DT, COL["gain"] + 5 * DT, COL["gain"] + 7 * DT]
OUT_PHASE = ["fox_out", "down0", "hgrn_out", "down1", "sb_out", "down2", "gla_out", "down3"]
PRE_SUM = [0, 2, 4, 6, 8, 9, 10, 11]
POST_SUM = [1, 3, 5, 7]
SUMMED = {q: n for n, q in enumerate([0, 1, 3, 5, 7, 9, 10, 11])}


def build(nc, io, stop=8):
    phases, n_units = plan_phases()
    order = list(phases)
    last_phase = OUT_PHASE[stop - 1]
    order = order[:order.index(last_phase) + 1]
    n_units = phases[last_phase].first + phases[last_phase].count
    following = {a: phases[b] for a, b in zip(order, order[1:])}

    with ExitStack() as ctx:
        sems = {}
        SHARED = {
            "gla_kdt": ("fx_turned", 2 * FOX_PAIRS), "gla_o": ("fx_pv", 2 * FOX_PAIRS), "gla_ds": ("fx_scores", 2 * FOX_PAIRS),
            "gla_kdh": ("fx_pth", 6 * FOX_PAIRS), "gla_kds": ("fx_pt", 2 * FOX_PAIRS), "gla_outh": ("fx_outh", 2 * FOX_PAIRS),
            "gla_out": ("fx_out", 2 * FOX_PAIRS), "gla_qh": ("fx_qh", 2 * FOX_PAIRS), "gla_qs": ("fx_qk", FOX_PAIRS),
            "gla_q": ("fx_kh", FOX_PAIRS), "gla_vs": ("fx_vs", FOX_PAIRS), "gla_vsh": ("fx_vsh", FOX_PAIRS),
            "gla_decay": ("fx_exp", 8 * FOX_PAIRS), "gla_diff": ("fx_max", 8 * FOX_PAIRS), "gla_cum": ("fx_c", 2 * FOX_PAIRS),
            "gla_rstd": ("fx_rsum", 2 * FOX_PAIRS), "gla_kd": ("fx_prob", 2 * FOX_PAIRS), "gla_low": ("fx_logit", 1),
            "gla_gate_hi": ("fx_gate_hi", 1), "gla_gate": ("fx_gate", 2), "gla_min": ("fx_setup", 7), "gla_abs": ("fx_ls", 3),
        }

        def sem(name):
            name = SHARED.get(name, (name,))[0]
            if name not in sems:
                sems[name] = ctx.enter_context(nc.semaphore(name))
            return sems[name]

        CREDITED = ("fx_out", "fx_turned", "hg_rstd", "hg_st", "hg_on", "hg_qe", "hg_lv", "hg_ms", "hg_lvl", "hg_scs", "hg_acc",
                    "hg_o", "hg_ds", "hg_sts", "hg_outh", "hg_out")

        def wait(eng, name, value):
            if isinstance(value, int) and value < 1:
                return
            of, base = SHARED.get(name, (name, 0))
            eng.wait_ge(sem(name), value + base + (of in CREDITED))

        place = [(nc.sbuf_base + 63) // 64 * 64]

        def fixed(name, shape, dt=F32, at=None):
            size = 4 * int(np.prod(shape[1:]))
            offset = place[0] if at is None else at
            if at is None:
                place[0] += (size + 31) // 32 * 32
            return nc.alloc_sbuf_tensor_at(name, shape, dt, offset=offset)

        h = fixed("h", [P, DT, T])
        at_x = place[0]
        x_hi = fixed("x_hi", [P, DT, T], F32R)
        x_lo = fixed("x_lo", [P, DT, T], F32R)
        y = fixed("y", [P, DT, T], at=at_x)
        xn = fixed("xn", [P, DT, T], at=at_x + 4 * DT * T)
        raw = fixed("raw", [P, RAW_SLOTS, DOWN_UNIT])
        w_hi = fixed("w_hi", [P, SPLIT_SLOTS, DOWN_UNIT], F32R)
        w_lo = fixed("w_lo", [P, SPLIT_SLOTS, DOWN_UNIT], F32R)
        cols = fixed("cols", [P, N_COLS])
        ident = fixed("ident", [P, P])
        ones = fixed("ones", [P, P])
        at_sq = place[0]
        sq = fixed("sq", [P, 2, T])
        sq_sum = fixed("sq_sum", [P, T])
        ln_ms = fixed("ln_ms", [P, T])
        rstd = fixed("rstd", [P, T])
        gated = fixed("gated", [P, 2, T], at=at_sq)
        silu = fixed("silu", [P, 2, T], at=at_sq + 8 * T)
        conv_a = fixed("conv_a", [P, T], at=at_sq + 16 * T)
        arena = place[0]
        arena_end = nc.sbuf_usable_end

        class Region:

            def __init__(self, tag):
                self.tag, self.at = tag, arena

            def take(self, name, shape, dt=F32, at=None):
                size = 4 * int(np.prod(shape[1:]))
                offset = self.at if at is None else at
                if at is None:
                    self.at += (size + 31) // 32 * 32
                    assert self.at <= arena_end, (self.tag, name, self.at - arena_end)
                t = nc.alloc_sbuf_tensor_at(f"{self.tag}_{name}", shape, dt, offset=offset)
                return t

        ps = [ctx.enter_context(nc.psum_tensor(f"bank{i}", [P, T], F32)) for i in range(8)]

        up = Region("up")
        a_hi = up.take("a_hi", [P, FT, T], F32R)
        a_lo = up.take("a_lo", [P, FT, T], F32R)
        conv_g = up.take("conv_g", [P, T])
        mix_at = arena
        mix_hi = nc.alloc_sbuf_tensor_at("mix_hi", [P, DT, T], F32R, offset=mix_at)
        mix_lo = nc.alloc_sbuf_tensor_at("mix_lo", [P, DT, T], F32R, offset=mix_at + 4 * DT * T)

        def mixer_region(tag):
            r = Region(tag)
            v = r.take("v", [P, DT * T])
            g = r.take("g", [P, DT * T])
            return r, v, g

        def u_of(name):
            return phases[name].first

        def convert_act(act, slot, u, size):
            act.wait_ge(sem(f"raw_ready{slot % 2}"), 8 * (u - slot % 2) + 16)
            act.wait_ge(sem("unit_used"), u + 1)
            nc.scalar.activation(w_hi[:, slot, 0:size], raw[:, slot % 2, 0:size], ACT.Copy).then_inc(sem("hi_ready"), 1)

        def convert_dve(dve, slot, u, size):
            dve.wait_ge(sem("hi_ready"), u + 1)
            nc.vector.tensor_tensor(w_lo[:, slot, 0:size], raw[:, slot % 2, 0:size],
                                    w_hi[:, slot, 0:size].bitcast(F32), ALU.subtract).then_inc(sem("split_ready"), 1)

        def ahead(convert, eng, name, c, u, last):
            slot = (c + 2) % 4
            if last and c >= 2:
                if name in following:
                    convert(eng, slot, following[name].first + c - 2, following[name].size)
            else:
                convert(eng, slot, u + 2, phases[name].size)

        def bodies(eng, name, body, first=0):
            n = phases[name].count // 4
            repeat(eng, first, n - 1, lambda j: body(j, 4 * j + phases[name].first, False))
            body(n - 1, 4 * (n - 1) + phases[name].first, True)

        CREDIT = 4

        def used(pe_or_other, u):
            pe_or_other.wait_ge(sem("unit_used"), u + 1 + CREDIT)

        def mm3(out, w, x, first, last):
            nc.tensor.matmul(out, w[0], x[0], start=first, stop=False)
            nc.tensor.matmul(out, w[0], x[1], start=False, stop=False)
            return nc.tensor.matmul(out, w[1], x[0], start=False, stop=last)

        def pe_unit_k(slot, bank, ks):
            for k in ks:
                ins = mm3(ps[bank][:], [w[:, slot, k * P:(k + 1) * P] for w in (w_hi, w_lo)],
                          [x_hi[:, k, :], x_lo[:, k, :]], k == 0, k == DT - 1)
                if k == DT - 1:
                    ins.then_inc(sem("unit_used"), 1)

        def pe_unit(pe, s, slot, u, bank):
            pe.wait_ge(sem("split_ready"), u + 1)
            pe_unit_k(slot, bank, range(DT))

        def pe_first_two(pe, s, u):
            pe.wait_ge(sem("split_ready"), u + 2)
            w = lambda part, c, k: part[:, c, k * P:(k + 1) * P]
            for k in range(DT):
                pe.wait_ge(sem("xhi_ready"), DT * s + k + 1)
                for c in range(2):
                    nc.tensor.matmul(ps[c][:], w(w_hi, c, k), x_hi[:, k, :], start=k == 0, stop=False)
                    nc.tensor.matmul(ps[c][:], w(w_lo, c, k), x_hi[:, k, :], start=False, stop=False)
            for k in range(DT):
                pe.wait_ge(sem("x_ready"), DT * s + k + 1)
                for c in range(2):
                    ins = nc.tensor.matmul(ps[c][:], w(w_hi, c, k), x_lo[:, k, :], start=False, stop=k == DT - 1)
                    if k == DT - 1:
                        ins.then_inc(sem("unit_used"), 1)

        def pe_tokens(pe, s, name, n0):
            for cb in range(phases[name].count // 2):
                c, u = 2 * (cb % 2), u_of(name) + 2 * cb
                pe.wait_ge(sem("split_ready"), u + 2)
                if cb == 0:
                    part = lambda w, k: w[:, c + k // 4, (k % 4) * 256:(k % 4 + 1) * 256]
                    for k in range(DT):
                        pe.wait_ge(sem("xhi_ready"), DT * s + k + 1)
                        for tt in range(TT):
                            x = x_hi[:, k, tt * P:(tt + 1) * P]
                            nc.tensor.matmul(ps[tt][:, 0:256], x, part(w_hi, k), start=k == 0, stop=False)
                            nc.tensor.matmul(ps[tt][:, 0:256], x, part(w_lo, k), start=False, stop=False)
                    for k in range(DT):
                        pe.wait_ge(sem("x_ready"), DT * s + k + 1)
                        for tt in range(TT):
                            ins = nc.tensor.matmul(ps[tt][:, 0:256], x_lo[:, k, tt * P:(tt + 1) * P], part(w_hi, k),
                                                   start=False, stop=k == DT - 1)
                            if k == DT - 1:
                                ins.then_inc(sem("tokens_done"), 1)
                for tt in range(TT):
                    if cb == 0:
                        continue
                    pe.wait_ge(sem("tokens_out"), n0 + 4 * (cb - 1) + tt + 1)
                    for k in range(DT):
                        at = (k % 4) * 256
                        ins = mm3(ps[tt][:, 0:256], [x[:, k, tt * P:(tt + 1) * P] for x in (x_hi, x_lo)],
                                  [w[:, c + k // 4, at:at + 256] for w in (w_hi, w_lo)], k == 0, k == DT - 1)
                    ins.then_inc(sem("tokens_done"), 1)
                pe.wait_ge(sem("tokens_done"), n0 + 4 * cb + 4)
                pe.sem_inc(sem("unit_used"), 2)

        def act_square(act, q, i, par, src):
            if q not in SUMMED:
                if i >= 2:
                    act.wait_ge(sem("sq_pe_summed"), 8 * (q // 2 - 1) + i - 1)
            elif not isinstance(i, int) or 9 * SUMMED[q] + i > 0:
                act.wait_ge(sem("sq_added"), 9 * SUMMED[q] + i)
            nc.scalar.activation(sq[:, par, :], src, ACT.Square).then_inc(sem("sq_ready"), 1)

        def dve_sum_start(dve, q):
            if q:
                dve.wait_ge(sem("ms_ready"), q)
            nc.vector.memset(sq_sum[:], 0.0).then_inc(sem("sq_added"), 1)

        def dve_square(dve, q, i, par):
            dve.wait_ge(sem("sq_ready"), 8 * q + i + 1)
            dve.wait_ge(sem("sq_added"), 9 * SUMMED[q] + i + 1)
            nc.vector.tensor_tensor(sq_sum[:], sq_sum[:], sq[:, par, :], ALU.add).then_inc(sem("sq_added"), 1)

        def pe_sum(pe, q):
            if q not in SUMMED:
                for i in range(DT):
                    pe.wait_ge(sem("sq_ready"), 8 * q + i + 1)
                    ins = nc.tensor.matmul(ps[7][:], ones[:], sq[:, i % 2, :], start=i == 0, stop=i == DT - 1)
                    ins.then_inc(sem("sq_pe_summed"), 1)
                pe.wait_ge(sem("sq_pe_summed"), 8 * (q // 2 - 1) + 8)
                pe.sem_inc(sem("ms_ready"), 1)
                return
            pe.wait_ge(sem("sq_added"), 9 * SUMMED[q] + 9)
            nc.tensor.matmul(ps[7][:], ones[:], sq_sum[:], start=True, stop=True).then_inc(sem("ms_ready"), 1)

        def act_rstd(act, q):
            act.wait_ge(sem("ms_ready"), q + 1)
            nc.scalar.activation(ln_ms[:], ps[7][:], ACT.Ln, bias=EPS, scale=1.0 / D).then_inc(sem("ln_ready"), 1)
            act.wait_ge(sem("ln_ready"), q + 1)
            nc.scalar.activation(rstd[:], ln_ms[:], ACT.Exp, scale=-0.5).then_inc(sem("rstd_ready"), 1)

        def norm_dve(dve, s):
            q = PRE_SUM[s]
            dve.wait_ge(sem("rstd_ready"), q + 1)
            for i in range(DT):
                g = PRE_GAIN[s] + i
                nc.vector.scalar_tensor_tensor(xn[:, i, :], h[:, i, :], cols[:, g:g + 1], rstd[:], ALU.mult,
                                               ALU.mult).then_inc(sem("xn_ready"), 1)
            for k in range(DT):
                dve.wait_ge(sem("xhi_ready"), DT * s + k + 1)
                nc.vector.tensor_tensor(x_lo[:, k, :], xn[:, k, :], x_hi[:, k, :].bitcast(F32),
                                        ALU.subtract).then_inc(sem("x_ready"), 1)

        def norm_act(act, s):
            for i in range(DT):
                act.wait_ge(sem("xn_ready"), DT * s + i + 1)
                nc.scalar.activation(x_hi[:, i, :], xn[:, i, :], ACT.Copy).then_inc(sem("xhi_ready"), 1)

        def tile_sum(s):
            return POST_SUM[s] if s < 4 else (PRE_SUM[s + 1] if s < stop - 1 else None)

        def tile_act(act, s, i, par, bank, u):
            if s < 4:
                used(act, u)
                nc.scalar.activation(y[:, i, :], ps[bank][:], ACT.Copy)
                act_square(act, tile_sum(s), i, par, ps[bank][:])
            elif tile_sum(s) is not None:
                act.wait_ge(sem("h_ready"), 8 * s + i + 1)
                act_square(act, tile_sum(s), i, par, h[:, i, :])

        def tile_dve(dve, s, i, par, bank, u):
            if s >= 4:
                used(dve, u)
                nc.vector.tensor_tensor(h[:, i, :], h[:, i, :], ps[bank][:], ALU.add).then_inc(sem("h_ready"), 1)
            if tile_sum(s) is not None:
                dve_square(dve, tile_sum(s), i, par)

        def bank_free(pe, s, i):
            if s < 4:
                pe.wait_ge(sem("sq_ready"), 8 * POST_SUM[s] + i - 1)
            else:
                pe.wait_ge(sem("h_ready"), 8 * s + i - 1)

        def end_pe(pe, s):
            if s < 4:
                pe_sum(pe, POST_SUM[s])
            if s < stop - 1:
                pe_sum(pe, PRE_SUM[s + 1])

        def end_act(act, s):
            if s < 4:
                act_rstd(act, POST_SUM[s])
                if s < stop - 1:
                    for i in range(DT):
                        act.wait_ge(sem("h_ready"), 8 * s + i + 1)
                        act_square(act, PRE_SUM[s + 1], i, i % 2, h[:, i, :])
            if s < stop - 1:
                act_rstd(act, PRE_SUM[s + 1])
                norm_act(act, s + 1)

        def end_dve(dve, s):
            if s < 4:
                dve.wait_ge(sem("rstd_ready"), POST_SUM[s] + 1)
                for i in range(DT + 1):
                    if i < DT:
                        g = POST_GAIN[s] + i
                        if i >= 2:
                            dve.wait_ge(sem("h_ready"), 8 * s + i - 1)
                        nc.vector.scalar_tensor_tensor(post_t[:, i % 2, :], y[:, i, :], cols[:, g:g + 1], rstd[:],
                                                       ALU.mult, ALU.mult).then_inc(sem("post_ready"), 1)
                    if 1 <= i <= DT:
                        k = i - 1
                        dve.wait_ge(sem("post_ready"), 8 * s + k + 1)
                        nc.vector.tensor_tensor(h[:, k, :], h[:, k, :], post_t[:, k % 2, :],
                                                ALU.add).then_inc(sem("h_ready"), 1)
            if s < stop - 1:
                norm_dve(dve, s + 1)

        post_t = nc.alloc_sbuf_tensor_at("post_t", [P, 2, T], F32, offset=arena)

        def pe_ffn(pe, s):
            f = s // 2
            def up_body(j, u, last, start=0):
                for c in range(start, 4):
                    pe.wait_ge(sem("gated_ready"), FT * f + 2 * j + c // 2 + 1)
                    pe_unit(pe, s, c, u + c, c)
            pe.wait_ge(sem("gated_ready"), FT * f + 1)
            pe_first_two(pe, s, u_of(f"up{f}"))
            up_body(0, u_of(f"up{f}"), False, start=2)
            bodies(pe, f"up{f}", up_body, first=1)
            pe.wait_ge(sem("gated_ready"), FT * f + FT - 1 + 2)

            def down_body(j, u, last):
                for c in range(4):
                    if c % 2 == 0:
                        bank_free(pe, s, 2 * j + c // 2)
                    pe.wait_ge(sem("split_ready"), u + c + 1)
                    pe.wait_ge(sem("a_ready"), FT * f + DOWN_BLOCKS * (c % 2 + 1))
                    for b in range(DOWN_BLOCKS):
                        k = DOWN_BLOCKS * (c % 2) + b
                        ins = mm3(ps[c // 2][:], [w[:, c, b * P:(b + 1) * P] for w in (w_hi, w_lo)],
                                  [a_hi[:, k, :], a_lo[:, k, :]], k == 0, k == FT - 1)
                    ins.then_inc(sem("unit_used"), 1)
            bodies(pe, f"down{f}", down_body)
            end_pe(pe, s)

        def act_ffn(act, s):
            f = s // 2
            def up_body(j, u, last):
                for p in range(2):
                    ft = 2 * j + p
                    n = FT * f + ft
                    ahead(convert_act, act, f"up{f}", 2 * p, u + 2 * p, last)
                    if f < 2:
                        act.wait_ge(sem("gated_ready"), n + 1)
                        used(act, u + 2 * p)
                        nc.scalar.activation(silu[:, p, :], ps[2 * p][:], ACT.Silu).then_inc(sem("silu_ready"), 1)
                    else:
                        m = FT * (f - 2) + ft
                        cb = COL[f"conv{f - 2}"]
                        act.wait_ge(sem("gated_ready"), n + 2)
                        for half, buf in enumerate((conv_a, conv_g)):
                            used(act, u + 2 * p + half)
                            idx = 2 * ft + half
                            nc.scalar.activation(buf[:], ps[2 * p + half][:], ACT.Identity,
                                                 bias=cols[:, bass.ds(cb + 6 * FT + idx, 1)],
                                                 scale=cols[:, bass.ds(cb + 4 * FT + idx, 1)]).then_inc(sem("tap_ready"), 1)
                        act.wait_ge(sem("conv_ready"), 2 * m + 1)
                        nc.scalar.activation(silu[:, p, :], conv_a[:], ACT.Silu).then_inc(sem("silu_ready"), 1)
                    ahead(convert_act, act, f"up{f}", 2 * p + 1, u + 2 * p + 1, last)
                    act.wait_ge(sem("gated_ready"), n + 1 + 2)
                    nc.scalar.activation(a_hi[:, ft, :], gated[:, p, :], ACT.Copy).then_inc(sem("ahi_ready"), 1)
            bodies(act, f"up{f}", up_body)
            exp_ln_table()

            def down_body(j, u, last):
                for c in range(4):
                    ahead(convert_act, act, f"down{f}", c, u + c, last)
                    if c % 2:
                        tile_act(act, s, 2 * j + c // 2, c // 2, c // 2, u + c)
            bodies(act, f"down{f}", down_body)
            end_act(act, s)

        def dve_ffn(dve, s):
            f = s // 2
            def up_body(j, u, last):
                for p in range(2):
                    ft = 2 * j + p
                    n = FT * f + ft
                    ahead(convert_dve, dve, f"up{f}", 2 * p, u + 2 * p, last)
                    if f >= 2:
                        m = FT * (f - 2) + ft
                        cb = COL[f"conv{f - 2}"]
                        for half, buf in enumerate((conv_a, conv_g)):
                            idx = 2 * ft + half
                            dve.wait_ge(sem("tap_ready"), 2 * m + half + 1)
                            nc.vector.scalar_tensor_tensor(buf[:, 1:T], ps[2 * p + half][:, 0:T - 1],
                                                           cols[:, bass.ds(cb + 2 * FT + idx, 1)], buf[:, 1:T],
                                                           ALU.mult, ALU.add).then_inc(sem("tap1_ready"), 1)
                            dve.wait_ge(sem("tap1_ready"), 2 * m + half + 1)
                            ins = nc.vector.scalar_tensor_tensor(buf[:, 2:T], ps[2 * p + half][:, 0:T - 2],
                                                                 cols[:, bass.ds(cb + idx, 1)], buf[:, 2:T],
                                                                 ALU.mult, ALU.add)
                            ins.then_inc(sem("conv_ready"), 1)
                    ahead(convert_dve, dve, f"up{f}", 2 * p + 1, u + 2 * p + 1, last)
                    dve.wait_ge(sem("silu_ready"), n + 1)
                    if f < 2:
                        used(dve, u + 2 * p + 1)
                        second = ps[2 * p + 1][:]
                    else:
                        dve.wait_ge(sem("conv_ready"), 2 * m + 2)
                        second = conv_g[:]
                    nc.vector.tensor_tensor(gated[:, p, :], silu[:, p, :], second, ALU.mult).then_inc(sem("gated_ready"), 1)
                    dve.wait_ge(sem("ahi_ready"), n + 1)
                    nc.vector.tensor_tensor(a_lo[:, ft, :], gated[:, p, :], a_hi[:, ft, :].bitcast(F32),
                                            ALU.subtract).then_inc(sem("a_ready"), 1)
            bodies(dve, f"up{f}", up_body)

            def down_body(j, u, last):
                for c in range(4):
                    ahead(convert_dve, dve, f"down{f}", c, u + c, last)
                    if c % 2:
                        tile_dve(dve, s, 2 * j + c // 2, c // 2, c // 2, u + c)
            if tile_sum(s) is not None:
                dve_sum_start(dve, tile_sum(s))
            bodies(dve, f"down{f}", down_body)
            end_dve(dve, s)

        early = {}

        def out_products(pe, name, c, slot_unit, ks, ready, first, last):
            pe.wait_ge(sem("split_ready"), slot_unit + 1)
            for k in ks:
                ready(pe, k)
                ins = mm3(ps[c % 2][:], [w[:, c, k * P:(k + 1) * P] for w in (w_hi, w_lo)],
                          [mix_hi[:, k, :], mix_lo[:, k, :]], first and k == ks[0], last and k == ks[-1])
            return ins

        def out_early(pe, name, c, ks, ready):
            done = early.setdefault((name, c), [])
            out_products(pe, name, c, u_of(name) + c, ks, ready, not done, False)
            done += ks

        def pe_out(pe, s, name, ready):
            def body(j, u, last):
                for c in range(4):
                    done = early.get((name, c), []) if isinstance(j, int) and j == 0 else []
                    bank_free(pe, s, 4 * j + c) if (s, j, c) > (0, 0, 1) else None
                    ks = [k for k in range(DT) if k not in done]
                    out_products(pe, name, c, u + c, ks, ready, not done, True).then_inc(sem("unit_used"), 1)
            bodies(pe, name, body)
            end_pe(pe, s)

        def act_out(act, s, name):
            def body(j, u, last):
                for c in range(4):
                    ahead(convert_act, act, name, c, u + c, last)
                    tile_act(act, s, 4 * j + c, c % 2, c % 2, u + c)
            bodies(act, name, body)
            end_act(act, s)

        def dve_out(dve, s, name):
            if tile_sum(s) is not None:
                dve_sum_start(dve, tile_sum(s))
            def body(j, u, last):
                for c in range(4):
                    ahead(convert_dve, dve, name, c, u + c, last)
                    tile_dve(dve, s, 4 * j + c, c % 2, c % 2, u + c)
            bodies(dve, name, body)
            end_dve(dve, s)

        def act_tokens(act, name, v_out, n0):
            n = phases[name].count // 4
            for j in range(n):
                for c in (0, 2):
                    cb = 2 * j + c // 2
                    u = u_of(name) + 4 * j + c
                    for tt in range(TT):
                        if tt == 0:
                            ahead(convert_act, act, name, c, u, j == n - 1)
                            ahead(convert_act, act, name, c + 1, u + 1, j == n - 1)
                        act.wait_ge(sem("tokens_done"), n0 + 4 * cb + tt + 1)
                        out = v_out(cb, tt)
                        src = ps[tt][:, 0:256]
                        if len(out.shape) == 3:
                            src = src.rearrange("p (a b) -> p a b", a=out.shape[1])
                        nc.scalar.activation(out, src, ACT.Copy).then_inc(sem("tokens_out"), 1)

        def dve_ahead_only(dve, name):
            n = phases[name].count // 4
            for j in range(n):
                for c in range(4):
                    ahead(convert_dve, dve, name, c, u_of(name) + 4 * j + c, j == n - 1)

        fx, fx_v, _ = mixer_region("fox")
        fv = fx_v[:].rearrange("p (m t c) -> p m t c", m=FOX_PAIRS, t=TT)
        q_hi = [fx.take(f"q{x}_hi", [P, T], F32R) for x in "ab"]
        q_lo = [fx.take(f"q{x}_lo", [P, T], F32R) for x in "ab"]
        k_hi = fx.take("k_hi", [P, T], F32R)
        k_lo = fx.take("k_lo", [P, T], F32R)
        NB = TT * (TT + 1) // 2 * P
        prob = fx.take("prob", [P, NB])
        pt_hi = fx.take("pt_hi", [P, NB], F32R)
        pt_lo = fx.take("pt_lo", [P, NB], F32R)
        c_left = fx.take("c_left", [P, T], F32R)
        c_right = fx.take("c_right", [P, T], F32R)
        c_head = fx.take("c_head", [P, T], F32R)
        vs_hi = fx.take("vs_hi", [P, TT, P], F32R)
        vs_lo = fx.take("vs_lo", [P, TT, P], F32R)
        negmask = fx.take("negmask", [P, P], F32R)
        ident_r = fx.take("ident_r", [P, P], F32R)
        neg_max = fx.take("neg_max", [P, 2, TT])
        sums = fx.take("sums", [P, 2, TT])
        rsums = fx.take("rsums", [P, 2, TT])
        gate_raw = fx.take("gate_raw", [P, IN_UNIT])
        gate_hi = fx.take("gate_hi", [P, IN_UNIT], F32R)
        gate_lo = fx.take("gate_lo", [P, IN_UNIT], F32R)
        g_abs, g_exp = prob[:, 0:T], prob[:, T:2 * T]
        fox_ones = nc.alloc_sbuf_tensor_at("fox_ones", [P, T], F32, offset=fx.at); fx.at += 4 * T
        log_f = nc.alloc_sbuf_tensor_at("fox_log_f", [P, T], F32, offset=fx.at); fx.at += 4 * T
        c_sum = nc.alloc_sbuf_tensor_at("fox_c", [P, T], F32, offset=fx.at); fx.at += 4 * T
        mask_raw = nc.alloc_sbuf_tensor_at("fox_mask_raw", [P, P], F32, offset=fx.at); fx.at += 4 * P
        assert fx.at <= arena_end, fx.at - arena_end

        S_BANK, S_AT = [3, 4, 3, 2], [3 * P, 0, 0, 0]
        PROB_AT = [0, P, 3 * P, 6 * P]
        T_BANK, T_AT = [5, 6, 7, 6], [0, 0, 0, 3 * P]
        PT_AT = [0, 4 * P, 8 * P, 7 * P]
        PT_PARTS = ((5, 0, 512, 0), (6, 0, 512, 512), (7, 0, 256, 1024))

        def scores_pe(pe, q_hi, q_lo, extra):
            for qt in range(TT):
                n, at = P * (qt + 1), S_AT[qt]
                sl = slice(qt * P, (qt + 1) * P)
                out = ps[S_BANK[qt]][:, at:at + n]
                mm3(out, [q_hi[:, sl], q_lo[:, sl]], [k_hi[:, 0:n], k_lo[:, 0:n]], True, False)
                if extra is not None:
                    nc.tensor.matmul(out, extra[0][:, sl], extra[1][:, 0:n], start=False, stop=False)
                ins = nc.tensor.matmul(ps[S_BANK[qt]][:, at + n - P:at + n], ident_r[:], negmask[:], start=False, stop=True)
            return ins

        def transpose_pe(pe, prob):
            for kt in range(TT):
                for qt in range(kt, TT):
                    at = T_AT[kt] + (qt - kt) * P
                    src = PROB_AT[qt] + kt * P
                    ins = nc.tensor.transpose(ps[T_BANK[kt]][:, at:at + P], prob[:, src:src + P], ident[:])
            return ins

        def values_pe(pe, bank):
            for kt in range(TT):
                n = T - kt * P
                sl = slice(PT_AT[kt], PT_AT[kt] + n)
                ins = mm3(ps[bank][:, kt * P:T], [vs_hi[:, kt, :], vs_lo[:, kt, :]], [pt_hi[:, sl], pt_lo[:, sl]],
                          kt == 0, kt == TT - 1)
            return ins

        def steps(eng, n, step):
            step(0, 0, True, False, False)
            step(1, 1, True, True, False)

            def two(j):
                step(2 * j, 0, True, True, False)
                step(2 * j + 1, 1, True, True, False)
            repeat(eng, 1, n // 2 - 1, two)
            step(n - 2, 0, True, True, False)
            step(n - 1, 1, True, True, True)
            step(n, 0, False, True, True)

        def pe_fox(pe):
            pe_tokens(pe, 0, "fox_v", 0)
            pe.wait_ge(sem("fx_gate"), 2)
            for k in range(DT):
                ins = mm3(ps[4][:], [w[:, k * P:(k + 1) * P] for w in (gate_hi, gate_lo)], [x_hi[:, k, :], x_lo[:, k, :]],
                          k == 0, k == DT - 1)
            ins.then_inc(sem("fx_logit"), 1)
            pe.wait_ge(sem("tokens_out"), 16)
            u0 = u_of("fox_qk")

            def out_ready(e, k):
                wait(e, "fx_out", 2 * (k + 1))

            def turn(head):
                wait(pe, "fx_prob", head + 1)
                wait(pe, "fx_out", head)
                transpose_pe(pe, prob).then_inc(sem("fx_turned"), 1)

            def bring(head):
                wait(pe, "fx_pt", head + 1)
                values_pe(pe, 7).then_inc(sem("fx_pv"), 1)

            def scores(head, hd):
                wait(pe, "fx_c", head + 1)
                wait(pe, "fx_exp", 4 * head)
                scores_pe(pe, q_hi[hd], q_lo[hd], (c_left, c_head)).then_inc(sem("fx_scores"), 1)

            def step(p, par, do_proj, do_mix, last):
                m = p - 1
                before = do_mix and not (isinstance(m, int) and m == 0)
                if do_mix:
                    wait(pe, "fx_qk", m + 1)
                    scores(2 * m, 0)
                if before:
                    turn(2 * m - 1)
                if do_proj:
                    pe_unit(pe, 0, 2 * par, u0 + 2 * p, 0)
                else:
                    out_early(pe, "fox_out", 0, list(range(6)), out_ready)
                if before:
                    bring(2 * m - 1)
                if do_mix:
                    scores(2 * m + 1, 1)
                    turn(2 * m)
                if do_proj:
                    pe_unit(pe, 0, 2 * par + 1, u0 + 2 * p + 1, 1)
                else:
                    out_early(pe, "fox_out", 1, list(range(6)), out_ready)
                if do_mix:
                    wait(pe, "fx_vs", m + 1)
                    bring(2 * m)
                    if not do_proj:
                        out_early(pe, "fox_out", 0, [6], out_ready)
                        turn(2 * m + 1)
                        out_early(pe, "fox_out", 1, [6], out_ready)
                        bring(2 * m + 1)
            steps(pe, FOX_PAIRS, step)
            pe_out(pe, 0, "fox_out", out_ready)

        ROWS = [slice(0, 64), slice(64, P)]

        def act_fox(act):
            act.wait_ge(sem("gate_loaded"), 16)
            nc.scalar.activation(gate_hi[:], gate_raw[:], ACT.Copy).then_inc(sem("fx_gate_hi"), 1)
            act_tokens(act, "fox_v", lambda cb, tt: fv[:, 2 * cb:2 * cb + 2, tt, :], 0)
            act.wait_ge(sem("fx_logit"), 1)
            b = cols[:, COL["fox_b"]:COL["fox_b"] + 1]
            nc.scalar.activation(g_abs, ps[4][:], ACT.Abs, bias=b).then_inc(sem("fx_ls"), 1)
            act.wait_ge(sem("fx_ls"), 1)
            nc.scalar.activation(g_exp, g_abs, ACT.Exp, scale=-1.0).then_inc(sem("fx_ls"), 1)
            act.wait_ge(sem("fx_ls"), 2)
            nc.scalar.activation(g_abs, g_exp, ACT.Ln, bias=1.0).then_inc(sem("fx_ls"), 1)
            u0 = u_of("fox_qk")

            def exps(head, hd):
                for qt, maxed in ((3, 1), (2, 3), (0, 3), (1, 4)):
                    act.wait_ge(sem("fx_max"), 4 * head + maxed)
                    if qt == 3 and not (isinstance(head, int) and head == 0):
                        wait(act, "fx_turned", head)
                    n = P * (qt + 1)
                    nc.scalar.activation(prob[:, PROB_AT[qt]:PROB_AT[qt] + n], ps[S_BANK[qt]][:, S_AT[qt]:S_AT[qt] + n],
                                         ACT.Exp, bias=neg_max[:, hd, qt:qt + 1],
                                         accum_out=sums[:, hd, qt:qt + 1]).then_inc(sem("fx_exp"), 1)

            def turned(head):
                wait(act, "fx_turned", head + 1)
                wait(act, "fx_pv", head)
                for bank, at, n, to in PT_PARTS:
                    nc.scalar.activation(pt_hi[:, to:to + n], ps[bank][:, at:at + n], ACT.Copy).then_inc(sem("fx_pth"), 1)

            def output(head, hd, m):
                act.wait_ge(sem("fx_pv"), head + 1)
                r = ROWS[hd]
                nc.scalar.activation(mix_hi[r, m, :], ps[7][r, :], ACT.Copy).then_inc(sem("fx_outh"), 1)

            def step(p, par, do_proj, do_mix, last):
                m = p - 1
                before = do_mix and not (isinstance(m, int) and m == 0)
                if do_mix:
                    exps(2 * m, 0)
                if before:
                    turned(2 * m - 1)
                if do_proj:
                    ahead(convert_act, act, "fox_qk", 2 * par, u0 + 2 * p, last)
                if before:
                    output(2 * m - 1, 1, m - 1)
                if do_mix:
                    exps(2 * m + 1, 1)
                    turned(2 * m)
                if do_proj:
                    used(act, u0 + 2 * p)
                    if do_mix:
                        act.wait_ge(sem("fx_scores"), 2 * m + 2)
                    for hd in range(2):
                        nc.scalar.activation(q_hi[hd][ROWS[hd], :], ps[0][ROWS[hd], :], ACT.Copy,
                                             scale=0.125).then_inc(sem("fx_qh"), 1)
                    ahead(convert_act, act, "fox_qk", 2 * par + 1, u0 + 2 * p + 1, last)
                    used(act, u0 + 2 * p + 1)
                    nc.scalar.activation(k_hi[:], ps[1][:], ACT.Copy).then_inc(sem("fx_kh"), 1)
                if do_mix:
                    output(2 * m, 0, m)
                    if not do_proj:
                        turned(2 * m + 1)
                        output(2 * m + 1, 1, m)
            steps(act, FOX_PAIRS, step)
            act_out(act, 0, "fox_out")

        def dve_fox(dve):
            for t in (q_hi, q_lo):
                nc.vector.memset(t[0][ROWS[1], :].bitcast(F32), 0.0)
                nc.vector.memset(t[1][ROWS[0], :].bitcast(F32), 0.0).then_inc(sem("fx_zero"), 1)
            nc.vector.memset(fox_ones[:], 1.0).then_inc(sem("fx_zero"), 1)
            dve.wait_ge(sem("fx_gate_hi"), 1)
            nc.vector.tensor_tensor(gate_lo[:], gate_raw[:], gate_hi[:].bitcast(F32), ALU.subtract).then_inc(sem("fx_gate"), 2)
            dve.wait_ge(sem("consts_loaded"), CONST_DMAS)
            nc.vector.tensor_copy(negmask[:], mask_raw[:]).then_inc(sem("fx_zero"), 1)
            nc.vector.tensor_copy(ident_r[:], ident[:]).then_inc(sem("fx_zero"), 1)
            dve_ahead_only(dve, "fox_v")
            b = cols[:, COL["fox_b"]:COL["fox_b"] + 1]
            dve.wait_ge(sem("fx_ls"), 1)
            nc.vector.tensor_scalar(c_sum[:], ps[4][:], b, 0.0, ALU.add, ALU.min).then_inc(sem("fx_setup"), 1)
            dve.wait_ge(sem("fx_setup"), 1)
            dve.wait_ge(sem("fx_ls"), 3)
            nc.vector.tensor_tensor(log_f[:], c_sum[:], g_abs, ALU.subtract).then_inc(sem("fx_setup"), 1)
            dve.wait_ge(sem("fx_setup"), 2)
            nc.vector.tensor_tensor_scan(c_sum[:], fox_ones[:], log_f[:], 0.0, ALU.mult, ALU.add).then_inc(sem("fx_setup"), 1)
            dve.wait_ge(sem("fx_setup"), 3)
            nc.vector.tensor_copy(c_head[:], c_sum[:]).then_inc(sem("fx_setup"), 1)
            dve.wait_ge(sem("fx_setup"), 4)
            nc.vector.tensor_tensor(c_left[:], c_sum[:], c_head[:].bitcast(F32), ALU.subtract).then_inc(sem("fx_setup"), 1)
            dve.wait_ge(sem("fx_setup"), 5)
            nc.vector.tensor_copy(c_right[32:64, :], c_left[32:64, :].bitcast(F32))
            nc.vector.tensor_copy(c_right[0:32, :], c_head[0:32, :].bitcast(F32))
            nc.vector.memset(c_right[64:P, :].bitcast(F32), 1.0).then_inc(sem("fx_setup"), 1)
            dve.wait_ge(sem("fx_setup"), 6)
            nc.vector.memset(c_left[0:64, :].bitcast(F32), -1.0)
            nc.vector.tensor_copy(c_left[64:96, :], c_head[64:96, :].bitcast(F32)).then_inc(sem("fx_setup"), 1)
            dve.wait_ge(sem("fx_setup"), 7)
            u0 = u_of("fox_qk")

            def forget(head):
                col = COL["onehot"] + head
                nc.vector.tensor_scalar(c_head[:], c_right[:].bitcast(F32), cols[:, bass.ds(col, 1)], None,
                                        ALU.mult).then_inc(sem("fx_c"), 1)

            def maxima(head, hd):
                dve.wait_ge(sem("fx_scores"), head + 1)
                for qt in (3, 2, 0, 1):
                    n = P * (qt + 1)
                    nc.vector.tensor_reduce(neg_max[:, hd, qt:qt + 1], ps[S_BANK[qt]][:, S_AT[qt]:S_AT[qt] + n], AX_X, ALU.max,
                                            negate=True).then_inc(sem("fx_max"), 1)

            def normalise(head, hd):
                dve.wait_ge(sem("fx_exp"), 4 * head + 4)
                nc.vector.reciprocal(rsums[:, hd, :], sums[:, hd, :]).then_inc(sem("fx_rsum"), 1)
                dve.wait_ge(sem("fx_rsum"), head + 1)
                for qt in range(TT):
                    sl = slice(PROB_AT[qt], PROB_AT[qt] + P * (qt + 1))
                    ins = nc.vector.tensor_scalar(prob[:, sl], prob[:, sl], rsums[:, hd, qt:qt + 1], None, ALU.mult)
                ins.then_inc(sem("fx_prob"), 1)

            def turned(head):
                for n_, (bank, at, n, to) in enumerate(PT_PARTS):
                    dve.wait_ge(sem("fx_pth"), 3 * head + n_ + 1)
                    ins = nc.vector.tensor_tensor(pt_lo[:, to:to + n], ps[bank][:, at:at + n],
                                                  pt_hi[:, to:to + n].bitcast(F32), ALU.subtract)
                ins.then_inc(sem("fx_pt"), 1)

            def output(head, hd, m):
                dve.wait_ge(sem("fx_outh"), head + 1)
                r = ROWS[hd]
                nc.vector.tensor_tensor(mix_lo[r, m, :], ps[7][r, :], mix_hi[r, m, :].bitcast(F32),
                                        ALU.subtract).then_inc(sem("fx_out"), 1)

            def step(p, par, do_proj, do_mix, last):
                m = p - 1
                before = do_mix and not (isinstance(m, int) and m == 0)
                if do_mix:
                    maxima(2 * m, 0)
                    forget(2 * m + 1)
                if before:
                    turned(2 * m - 1)
                if do_mix:
                    normalise(2 * m, 0)
                if do_proj:
                    ahead(convert_dve, dve, "fox_qk", 2 * par, u0 + 2 * p, last)
                if before:
                    output(2 * m - 1, 1, m - 1)
                if do_mix:
                    maxima(2 * m + 1, 1)
                    if do_proj:
                        forget(2 * m + 2)
                    turned(2 * m)
                    normalise(2 * m + 1, 1)
                if do_proj:
                    for hd in range(2):
                        r = ROWS[hd]
                        dve.wait_ge(sem("fx_qh"), 2 * p + hd + 1)
                        nc.vector.scalar_tensor_tensor(q_lo[hd][r, :], ps[0][r, :], 0.125, q_hi[hd][r, :].bitcast(F32),
                                                       ALU.mult, ALU.subtract)
                    dve.wait_ge(sem("fx_kh"), p + 1)
                    nc.vector.tensor_tensor(k_lo[:], ps[1][:], k_hi[:].bitcast(F32), ALU.subtract).then_inc(sem("fx_qk"), 1)
                    ahead(convert_dve, dve, "fox_qk", 2 * par + 1, u0 + 2 * p + 1, last)
                if do_mix:
                    output(2 * m, 0, m)
                    if not do_proj:
                        turned(2 * m + 1)
                        output(2 * m + 1, 1, m)
            forget(0)
            steps(dve, FOX_PAIRS, step)
            dve_out(dve, 0, "fox_out")

        def pool_fox(pool):
            pool.wait_ge(sem("tokens_out"), 16)

            def stage(m, first):
                if not first:
                    pool.wait_ge(sem("fx_pv"), 2 * m)
                nc.gpsimd.tensor_copy(vs_hi[:], fv[:, m, :, :]).then_inc(sem("fx_vsh"), 1)
                pool.wait_ge(sem("fx_vsh"), m + 1)
                nc.gpsimd.tensor_tensor(vs_lo[:], fv[:, m, :, :], vs_hi[:].bitcast(F32),
                                        ALU.subtract).then_inc(sem("fx_vs"), 1)
            for m in range(FOX_PAIRS):
                stage(m, m == 0)

        def pe_gates(pe, s, name, n0):
            for i in range(phases[name].count):
                if i >= 4:
                    pe.wait_ge(sem("gates_out"), n0 + i - 3)
                pe_unit(pe, s, i % 4, u_of(name) + i, i % 4)

        def act_gates(act, name, g_out):
            n = phases[name].count
            for i in range(n):
                ahead(convert_act, act, name, i % 4, u_of(name) + i, i >= n - 4)
                used(act, u_of(name) + i)
                nc.scalar.activation(g_out[:, i, :], ps[i % 4][:], ACT.Silu).then_inc(sem("gates_out"), 1)
            exp_ln_table()

        def stage(pool, v, vs, m, tag, used_name, used_per):
            wait(pool, used_name, used_per * m)
            nc.gpsimd.tensor_copy(vs[0][:], v[:, m, :, :]).then_inc(sem(tag + "_vsh"), 1)
            wait(pool, tag + "_vsh", m + 1)
            nc.gpsimd.tensor_tensor(vs[1][:], v[:, m, :, :], vs[0][:].bitcast(F32),
                                    ALU.subtract).then_inc(sem(tag + "_vs"), 1)

        def stage_values(pool, v, vs, n, tag, n_out, used_name, used_per):
            pool.wait_ge(sem("tokens_out"), n_out)
            for m in range(n):
                stage(pool, v, vs, m, tag, used_name, used_per)

        def exp_ln_table():
            nc.scalar.preload_act_table_set("natural_log_exp_and_others")

        B = [sq[:, 0, :], sq[:, 1, :], sq_sum[:], ln_ms[:], rstd[:]]

        hg, hg_v, hg_g = mixer_region("hgrn")
        hv = hg_v[:].rearrange("p (m t c) -> p m t c", m=8, t=TT)
        hgate = hg_g[:].rearrange("p (m t) -> p m t", m=8)
        hq = hg.take("q", [P, T])
        hk = hg.take("k", [P, T])
        hb = hg.take("b", [P, T])
        lx = [[hg.take(f"l{i}_{x}", [P, T], F32R) for x in ("hi", "lo")] for i in range(2)]
        sc = hg.take("scores", [P, T])
        scs = [hg.take(f"sc_{x}", [P, T], F32R) for x in ("hi", "lo")]
        hvs = [hg.take(f"vs_{x}", [P, TT, P], F32R) for x in ("hi", "lo")]
        qe = [hg.take(f"qe_{x}", [P, T], F32R) for x in ("hi", "lo")]
        kd = [hg.take(f"kd_{x}", [P, 2, TT, P], F32R) for x in ("hi", "lo")]
        st = hg.take("st", [P, NCH, P])
        sts = [hg.take(f"st_{x}", [P, NCH, P], F32R) for x in ("hi", "lo")]
        lv_mask = hg.take("lv_mask", [P, 4, P], U32)
        scan_mask = hg.take("scan_mask", [P, T])
        dec = hg.take("dec", [P, NCH])
        lbt = hg.take("lbt", [P, 8, DT])
        sg0, sg1 = B[0], B[1]
        dl = [B[2], B[3]]
        pr = [B[4], hg.take("pr1", [P, T])[:]]
        ho, hr = (hg.take(n, [P, T])[:] for n in ("ho", "hr"))

        def halves(t, l):
            return t.rearrange("p (g x y) -> p g x y", x=2, y=32 >> l)

        def steps4(eng, step):
            step(0, 0, True, False, False, False, False)
            step(1, 1, True, True, False, False, False)
            step(2, 0, True, True, True, False, False)

            def two(j):
                step(2 * j + 1, 1, True, True, True, True, False)
                step(2 * j + 2, 0, True, True, True, True, False)
            repeat(eng, 1, 3, two)
            step(7, 1, True, True, True, True, True)
            step(8, 0, False, True, True, True, True)
            step(9, 1, False, False, True, True, True)
            step(10, 0, False, False, False, True, True)

        def less_middle(ve, out, l):
            if l == 3:
                v = lambda t: t.rearrange("p (g x) -> p g x", x=8)
                return ve.tensor_tensor(v(out), v(hb[:]), v(hb[:])[:, :, 3:4].to_broadcast([P, T // 8, 8]), ALU.subtract)
            b_, d_, half = halves(hb[:], l), halves(out, l), 32 >> l
            ref = b_[:, :, 0, half - 1:half].to_broadcast([P, T // (2 * half), half])
            ve.tensor_tensor(d_[:, :, 1, :], b_[:, :, 1, :], ref, ALU.subtract)
            return ve.tensor_tensor(d_[:, :, 0, :], ref, b_[:, :, 0, :], ALU.subtract)

        def pe_turn_kd(pe, bank, src):
            for tt in range(TT):
                ins = nc.tensor.transpose(ps[bank][:, tt * P:(tt + 1) * P], src[:, tt * P:(tt + 1) * P], ident[:])
            return ins

        def pe_hgrn(pe):
            pe_tokens(pe, 2, "hgrn_v", 16)
            pe.wait_ge(sem("tokens_out"), 32)
            pe_gates(pe, 2, "hgrn_g", 0)
            pe.wait_ge(sem("gates_out"), 8)
            u0 = u_of("hgrn_qf")

            def level(m, l):
                wait(pe, "hg_lvl", 4 * m + l + 1)
                wait(pe, "hg_acc", 4 * m + l - 1)
                key, query = (lx[0], lx[1]) if l == 3 else (lx[l % 2], lx[l % 2])
                for tt in range(TT):
                    sl = slice(tt * P, (tt + 1) * P)
                    ins = mm3(ps[2 + l % 2][:, sl], [x[:, sl] for x in key], [x[:, sl] for x in query], True, True)
                ins.then_inc(sem("hg_lv"), 1)

            def out_ready(e, k):
                wait(e, "hg_out", k + 1)

            def step(p, par, do_proj, do_levels, do_out, do_norm, last):
                m, b, o = p - 1, p - 2, p - 3
                final = isinstance(p, int) and p
                if do_proj:
                    wait(pe, "hg_q", p)
                    pe_unit(pe, 2, 2 * par, u0 + 2 * p, 0)
                if final == 8:
                    wait(pe, "hg_q", 8)
                    out_early(pe, "hgrn_out", 0, [0, 1, 2, 3, 4], out_ready)
                if final == 10:
                    out_early(pe, "hgrn_out", 1, [5], out_ready)
                    out_early(pe, "hgrn_out", 0, [6], out_ready)
                if do_out:
                    wait(pe, "hg_kds", b + 1)
                    wait(pe, "hg_vs", b + 1)
                    wait(pe, "hg_st", 7 * b)
                    for c in range(NCH - 1):
                        out = ps[5 + c // 4][:, (c % 4) * P:(c % 4 + 1) * P]
                        ins = mm3(out, [x[:, c % 2, c // 2, :] for x in kd], [x[:, c // 2, :] for x in hvs], True, True)
                    ins.then_inc(sem("hg_ds"), 1)
                if do_norm:
                    wait(pe, "hg_sq", o + 1)
                    nc.tensor.matmul(ps[4][:], ones[:], ho, start=True, stop=True).then_inc(sem("hg_ms"), 1)
                if do_proj:
                    wait(pe, "hg_fl", p)
                    pe_unit(pe, 2, 2 * par + 1, u0 + 2 * p + 1, 1)
                if final == 9:
                    wait(pe, "hg_fl", 8)
                    out_early(pe, "hgrn_out", 1, [0, 1, 2, 3, 4], out_ready)
                    out_early(pe, "hgrn_out", 0, [5], out_ready)
                if do_levels:
                    level(m, 0)
                    level(m, 1)
                if do_out:
                    wait(pe, "hg_scs", b + 1)
                    wait(pe, "hg_qes", b + 1)
                    wait(pe, "hg_sts", b + 1)
                    wait(pe, "hg_on", b)
                    for tt in range(TT):
                        mm3(ps[7][:, tt * P:(tt + 1) * P], [x[:, tt, :] for x in hvs], [x[:, tt * P:(tt + 1) * P] for x in scs],
                            True, False)
                        for c in (2 * tt, 2 * tt + 1):
                            if c:
                                sl = slice(c * CHUNK, (c + 1) * CHUNK)
                                ins = mm3(ps[7][:, sl], [x[:, c, :] for x in sts], [x[:, sl] for x in qe], False, c == 2 * tt + 1)
                    ins.then_inc(sem("hg_o"), 1)
                if do_levels:
                    level(m, 2)
                    level(m, 3)
                if do_levels:
                    wait(pe, "hg_kd", m + 1)
                    wait(pe, "hg_kds", m)
                    wait(pe, "hg_rstd", 2 * b - 1)
                    pe_turn_kd(pe, 4, pr[0]).then_inc(sem("hg_kdt"), 1)
            steps4(pe, step)
            pe_out(pe, 2, "hgrn_out", out_ready)

        def act_hgrn(act):
            act.wait_ge(sem("hg_lb"), 1)
            nc.scalar.activation(lbt[:, 1:4, :], lbt[:, 1:4, :], ACT.Exp).then_inc(sem("hg_lbe"), 1)
            act_tokens(act, "hgrn_v", lambda cb, tt: hv[:, 2 * cb:2 * cb + 2, tt, :], 16)
            act_gates(act, "hgrn_g", hgate)
            u0 = u_of("hgrn_qf")

            def step(p, par, do_proj, do_levels, do_out, do_norm, last):
                m, b, o = p - 1, p - 2, p - 3
                ex = lambda out, src, name, **k: nc.scalar.activation(out, src, ACT.Exp, **k).then_inc(sem(name), 1)
                cp = lambda out, src, name: nc.scalar.activation(out, src, ACT.Copy).then_inc(sem(name), 1)
                c0 = lambda: ahead(convert_act, act, "hgrn_qf", 2 * par, u0 + 2 * p, last) if do_proj else None
                c1 = lambda: ahead(convert_act, act, "hgrn_qf", 2 * par + 1, u0 + 2 * p + 1, last) if do_proj else None

                def kd_hi(half):
                    wait(act, "hg_kdt", b + 1)
                    wait(act, "hg_ds", b)
                    cp(kd[0][ROWS[half], half, :, :], ps[4][ROWS[half], :].rearrange("p (t c) -> p t c", t=TT), "hg_kdh")

                def level_hi(n, l, to, src):
                    wait(act, "hg_pr", 5 * m + n + 1)
                    wait(act, "hg_lv", 4 * m + l)
                    cp(to[0][:], src, "hg_prh")
                if do_levels:
                    used(act, u0 + 2 * m)
                    wait(act, "hg_qe", m)
                    cp(hq[:], ps[0][:], "hg_q")
                    wait(act, "hg_fl", m + 1)
                    wait(act, "hg_dec", m)
                    ex(sg1, sg0, "hg_sig", scale=-1.0)
                if do_norm:
                    wait(act, "hg_o", o + 1)
                    wait(act, "hg_outh", o)
                    wait(act, "hg_out", o)
                    nc.scalar.activation(ho, ps[7][:], ACT.Square).then_inc(sem("hg_sq"), 1)
                if do_levels:
                    wait(act, "hg_sig", 3 * m + 1)
                    nc.scalar.activation(sg0, sg1, ACT.Ln, bias=1.0).then_inc(sem("hg_sig"), 1)
                if do_levels:
                    wait(act, "hg_sig", 3 * m + 2)
                    ex(sg1, sg0, "hg_sig", scale=-1.0)
                if do_out:
                    kd_hi(0)
                    kd_hi(1)
                if do_levels:
                    wait(act, "hg_f", m + 1)
                    nc.scalar.activation(sg0, dl[0], ACT.Ln).then_inc(sem("hg_lf"), 1)
                if do_out:
                    wait(act, "hg_acc", 4 * b + 4)
                    wait(act, "hg_o", b)
                    cp(scs[0][:], sc[:], "hg_sch")
                c0()
                if do_levels:
                    wait(act, "hg_d0", m + 1)
                    ex(dl[0], dl[0], "hg_e")
                    wait(act, "hg_d", 4 * m + 1)
                    ex(dl[1], dl[1], "hg_e")
                    level_hi(0, 0, lx[0], pr[0])
                    level_hi(1, 0, lx[1], pr[1])
                if do_levels:
                    wait(act, "hg_d", 4 * m + 2)
                    ex(dl[0], dl[0], "hg_e")
                if do_out:
                    wait(act, "hg_st", 7 * b + 7)
                    wait(act, "hg_o", b)
                    cp(sts[0][:, 1:NCH, :], st[:, 1:NCH, :], "hg_sth")
                if do_norm:
                    wait(act, "hg_ms", o + 1)
                    wait(act, "hg_on", o)
                    nc.scalar.activation(hr, ps[4][:], ACT.Ln, bias=EPS, scale=1.0 / P).then_inc(sem("hg_rstd"), 1)
                if do_norm:
                    wait(act, "hg_rstd", 2 * o + 1)
                    ex(hr, hr, "hg_rstd", scale=-0.5)
                if do_levels:
                    wait(act, "hg_d", 4 * m + 3)
                    wait(act, "hg_lfc", m + 1)
                    ex(sg0, dl[1], "hg_e3", scale=-1.0)
                    wait(act, "hg_e3", m + 1)
                    ex(dl[1], dl[1], "hg_e")
                    level_hi(2, 1, lx[0], pr[0])
                    wait(act, "hg_b", m + 1)
                    ex(sg1, hb[:], "hg_eb")
                c1()
                if do_levels:
                    level_hi(3, 2, lx[1], pr[1])
                if do_norm:
                    wait(act, "hg_og", o + 1)
                    cp(mix_hi[:, o, :], ho, "hg_outh")
                if do_levels:
                    wait(act, "hg_d", 4 * m + 4)
                    ex(dl[0], dl[0], "hg_ed")
                    level_hi(4, 3, lx[0], pr[0])
                if do_levels:
                    wait(act, "hg_qe", m + 1)
                    wait(act, "hg_o", m)
                    cp(qe[0][:], pr[1], "hg_qeh")
            steps4(act, step)
            act_out(act, 2, "hgrn_out")

        def dve_hgrn(dve):
            lt = COL["lb_table"]
            row = lambda r: cols[:, lt + r * DT:lt + (r + 1) * DT]
            dve.wait_ge(sem("x_ready"), 8 * 2 + 8)
            n = [0]

            def link(ins, name="hg_setup"):
                n[0] += 1
                ins.then_inc(sem(name), 1)
                dve.wait_ge(sem(name), n[0])
            link(nc.vector.tensor_tensor(lbt[:, 0, :], row(0), row(1), ALU.max))
            link(nc.vector.tensor_tensor(lbt[:, 0, :], lbt[:, 0, :], row(2), ALU.max))
            for r in range(3):
                ins = nc.vector.tensor_tensor(lbt[:, 1 + r, :], row(r), lbt[:, 0, :], ALU.subtract)
            ins.then_inc(sem("hg_lb"), 1)
            for t in kd:
                nc.vector.memset(t[ROWS[1], 0, :, :].bitcast(F32), 0.0)
                nc.vector.memset(t[ROWS[0], 1, :, :].bitcast(F32), 0.0)
            link(nc.vector.memset(sc[:], 0.0))
            dve.wait_ge(sem("hg_lbe"), 1)
            link(nc.vector.tensor_tensor(lbt[:, 6, :], lbt[:, 1, :], lbt[:, 2, :], ALU.add))
            link(nc.vector.tensor_tensor(lbt[:, 4, :], lbt[:, 6, :], lbt[:, 3, :], ALU.add))
            link(nc.vector.reciprocal(lbt[:, 5, :], lbt[:, 4, :]))
            link(nc.vector.tensor_tensor(lbt[:, 6, :], lbt[:, 6, :], lbt[:, 5, :], ALU.mult))
            link(nc.vector.tensor_scalar(lbt[:, 7, :], lbt[:, 6, :], -1.0, 1.0, ALU.mult, ALU.add))
            dve_ahead_only(dve, "hgrn_v")
            dve_ahead_only(dve, "hgrn_g")
            dve.wait_ge(sem("hg_consts"), 32)
            u0 = u_of("hgrn_qf")

            def step(p, par, do_proj, do_levels, do_out, do_norm, last):
                m, b, o = p - 1, p - 2, p - 3
                tt_ = lambda out, a, c, op, name: nc.vector.tensor_tensor(out, a, c, op).then_inc(sem(name), 1)
                c0 = lambda: ahead(convert_dve, dve, "hgrn_qf", 2 * par, u0 + 2 * p, last) if do_proj else None
                c1 = lambda: ahead(convert_dve, dve, "hgrn_qf", 2 * par + 1, u0 + 2 * p + 1, last) if do_proj else None

                def take(head, l):
                    nc.vector.copy_predicated(sc[:].rearrange("p (t c) -> p t c", t=TT),
                                              lv_mask[:, l:l + 1, :].to_broadcast([P, TT, P]),
                                              ps[2 + l % 2][:].rearrange("p (t c) -> p t c", t=TT)).then_inc(sem("hg_acc"), 1)

                def product(l):
                    wait(dve, "hg_e", 4 * m + l + 1)
                    out, e_ = halves(pr[l % 2], l), halves(dl[l % 2], l)
                    nc.vector.tensor_tensor(out[:, :, 1, :], halves(hq[:], l)[:, :, 1, :], e_[:, :, 1, :], ALU.mult)
                    tt_(out[:, :, 0, :], halves(hk[:], l)[:, :, 0, :], e_[:, :, 0, :], ALU.mult, "hg_pr")

                def level_lo(n, to, src, name="hg_lvl"):
                    wait(dve, "hg_prh", 5 * m + n + 1)
                    ins = nc.vector.tensor_tensor(to[1][:], src, to[0][:].bitcast(F32), ALU.subtract)
                    ins.then_inc(sem(name), 1)

                def f_and_k():
                    wait(dve, "hg_sig", 3 * m + 3)
                    wait(dve, "hg_kd", m)
                    lb = [lbt[:, r, bass.ds(m, 1)] for r in (6, 7)]
                    nc.vector.tensor_scalar(dl[0], sg1, lb[1], lb[0], ALU.mult, ALU.add).then_inc(sem("hg_f"), 1)
                    wait(dve, "hg_f", m + 1)
                    nc.vector.tensor_scalar(hk[:], dl[0], -1.0, 1.0, ALU.mult, ALU.add).then_inc(sem("hg_k"), 1)
                if do_levels:
                    used(dve, u0 + 2 * m + 1)
                    wait(dve, "hg_pr", 5 * m)
                    nc.vector.tensor_scalar(sg0, ps[1][:], -80.0, None, ALU.max).then_inc(sem("hg_fl"), 1)
                if do_out:
                    wait(dve, "hg_lv", 4 * b + 4)
                    wait(dve, "hg_ds", b)
                    wait(dve, "hg_acc", 4 * b + 3)
                    for half in range(2):
                        wait(dve, "hg_kdh", 2 * b + half + 1)
                        r = ROWS[half]
                        ins = nc.vector.tensor_tensor(kd[1][r, half, :, :], ps[4][r, :].rearrange("p (t c) -> p t c", t=TT),
                                                      kd[0][r, half, :, :].bitcast(F32), ALU.subtract)
                        if half == 0:
                            take(b, 3)
                    ins.then_inc(sem("hg_kds"), 1)
                if do_levels:
                    f_and_k()
                if do_out:
                    wait(dve, "hg_qeh", b + 1)
                    wait(dve, "hg_o", b)
                    tt_(qe[1][:], pr[1], qe[0][:].bitcast(F32), ALU.subtract, "hg_qes")
                if do_levels:
                    wait(dve, "hg_lf", m + 1)
                    nc.vector.tensor_scalar(sg1, sg0, LOG_F_MIN, None, ALU.max).then_inc(sem("hg_lfc"), 1)
                    wait(dve, "hg_lfc", m + 1)
                    wait(dve, "hg_eb", m)
                    wait(dve, "hg_d", 4 * m)
                    nc.vector.tensor_tensor_scan(hb[:], scan_mask[:], sg1, 0.0, ALU.mult, ALU.add).then_inc(sem("hg_b"), 1)
                    wait(dve, "hg_b", m + 1)
                    wait(dve, "hg_k", m + 1)
                    less_middle(nc.vector, dl[0], 0).then_inc(sem("hg_d0"), 1)
                if do_levels:
                    wait(dve, "hg_q", m + 1)
                    wait(dve, "hg_kdt", m)
                    product(0)
                if do_levels:
                    wait(dve, "hg_qes", m)
                    product(1)
                    wait(dve, "hg_lv", 4 * m)
                    level_lo(0, lx[0], pr[0])
                if do_out:
                    wait(dve, "hg_sch", b + 1)
                    tt_(scs[1][:], sc[:], scs[0][:].bitcast(F32), ALU.subtract, "hg_scs")
                if do_levels:
                    level_lo(1, lx[1], pr[1])
                if do_out:
                    wait(dve, "hg_ds", b + 1)
                    wait(dve, "hg_dec", b + 1)
                    wait(dve, "hg_sts", b)
                    for c in range(1, NCH):
                        ds_ = ps[5 + (c - 1) // 4][:, ((c - 1) % 4) * P:((c - 1) % 4 + 1) * P]
                        if c == 1:
                            nc.vector.tensor_copy(st[:, 1, :], ds_).then_inc(sem("hg_st"), 1)
                        else:
                            wait(dve, "hg_st", 7 * b + c - 1)
                            nc.vector.scalar_tensor_tensor(st[:, c, :], st[:, c - 1, :], dec[:, c - 1:c], ds_, ALU.mult,
                                                           ALU.add).then_inc(sem("hg_st"), 1)
                if do_levels:
                    wait(dve, "hg_lvl", 4 * m + 1)
                    product(2)
                c0()
                if do_out:
                    wait(dve, "hg_sth", b + 1)
                    tt_(sts[1][:, 1:NCH, :], st[:, 1:NCH, :], sts[0][:, 1:NCH, :].bitcast(F32), ALU.subtract, "hg_sts")
                if do_norm:
                    wait(dve, "hg_rstd", 2 * o + 2)
                    g = COL["hgrn_norm"]
                    nc.vector.scalar_tensor_tensor(ho, ps[7][:], cols[:, g:g + 1], hr, ALU.mult, ALU.mult).then_inc(sem("hg_on"), 1)
                if do_levels:
                    wait(dve, "hg_lv", 4 * m + 1)
                    wait(dve, "hg_scs", m)
                    level_lo(2, lx[0], pr[0])
                    take(m, 0)
                    wait(dve, "hg_e", 4 * m + 4)
                    wait(dve, "hg_lvl", 4 * m + 2)
                    tt_(pr[1], hq[:], dl[1], ALU.mult, "hg_pr")
                    wait(dve, "hg_e3", m + 1)
                    wait(dve, "hg_lvl", 4 * m + 3)
                    tt_(pr[0], hk[:], sg0, ALU.mult, "hg_pr")
                if do_norm:
                    wait(dve, "hg_on", o + 1)
                    tt_(ho, ho, hgate[:, o, :], ALU.mult, "hg_og")
                c1()
                if do_levels:
                    wait(dve, "hg_lv", 4 * m + 2)
                    wait(dve, "hg_acc", 4 * m + 1)
                    level_lo(3, lx[1], pr[1], "hg_lq")
                    take(m, 1)
                if do_norm:
                    wait(dve, "hg_outh", o + 1)
                    tt_(mix_lo[:, o, :], ho, mix_hi[:, o, :].bitcast(F32), ALU.subtract, "hg_out")
                if do_levels:
                    wait(dve, "hg_lv", 4 * m + 3)
                    wait(dve, "hg_acc", 4 * m + 2)
                    level_lo(4, lx[0], pr[0])
                    v = lambda t: t.rearrange("p (g x) -> p g x", x=CHUNK)
                    wait(dve, "hg_ed", m + 1)
                    wait(dve, "hg_lvl", 4 * m + 4)
                    tt_(pr[0], hk[:], dl[0], ALU.mult, "hg_kd")
                    wait(dve, "hg_eb", m + 1)
                    wait(dve, "hg_lq", m + 1)
                    tt_(pr[1], hq[:], sg1, ALU.mult, "hg_qe")
                    take(m, 2)
                    wait(dve, "hg_st", 7 * m)
                    nc.vector.tensor_copy(dec[:], v(sg1)[:, :, CHUNK - 1]).then_inc(sem("hg_dec"), 1)
            steps4(dve, step)
            dve_out(dve, 2, "hgrn_out")

        def pool_hgrn(pool):
            pool.wait_ge(sem("x_ready"), 8 * 2 + 1)
            nc.gpsimd.dma_start(lv_mask[:], io["lv_mask"]).then_inc(sem("hg_consts"), 16)
            nc.gpsimd.dma_start(scan_mask[:], io["scan_mask"]).then_inc(sem("hg_consts"), 16)
            pool.wait_ge(sem("tokens_out"), 32)

            def head(m):
                wait(pool, "hg_b", m + 1)
                wait(pool, "hg_pr", 5 * m)
                less_middle(nc.gpsimd, dl[1], 1).then_inc(sem("hg_d"), 1)
                wait(pool, "hg_pr", 5 * m + 1)
                less_middle(nc.gpsimd, dl[0], 2).then_inc(sem("hg_d"), 1)
                wait(pool, "hg_pr", 5 * m + 2)
                less_middle(nc.gpsimd, dl[1], 3).then_inc(sem("hg_d"), 1)
                wait(pool, "hg_pr", 5 * m + 3)
                v = lambda t: t.rearrange("p (g x) -> p g x", x=CHUNK)
                last_b = v(hb[:])[:, :, CHUNK - 1:CHUNK].to_broadcast([P, NCH, CHUNK])
                nc.gpsimd.tensor_tensor(v(dl[0]), last_b, v(hb[:]), ALU.subtract).then_inc(sem("hg_d"), 1)
                stage(pool, hv, hvs, m, "hg", "hg_o", 1)
            for m in range(8):
                head(m)

        sb, sb_v, _ = mixer_region("sb")
        sv = sb_v[:, 0:4 * T].rearrange("p (m t c) -> p m t c", m=4, t=TT)
        sq_hi = [sb.take(f"q{x}_hi", [P, T], F32R) for x in "ab"]
        sq_lo = [sb.take(f"q{x}_lo", [P, T], F32R) for x in "ab"]
        sk_hi = sb.take("k_hi", [P, T], F32R)
        sk_lo = sb.take("k_lo", [P, T], F32R)
        s_abs = [sb.take("abs_a", [P, NB])]
        s_sum = sb.take("sum", [P, NB])
        s_prob = sb.take("prob", [P, NB])
        spt_hi = sb.take("pt_hi", [P, NB], F32R)
        spt_lo = sb.take("pt_lo", [P, NB], F32R)
        svs = [sb.take(f"vs_{x}", [P, TT, P], F32R) for x in ("hi", "lo")]
        s_neg = sb.take("negmask", [P, P], F32R)
        s_ident = sb.take("ident_r", [P, P], F32R)
        s_ones = sb.take("ones", [P, T])
        s_block = sb.take("block_ones", [P, P])
        qraw = sb.take("qraw", [P, T])
        kraw = sb.take("kraw", [P, T])
        px = nc.alloc_sbuf_tensor_at("pool_x", [P, 4, T], F32, offset=sb.at); sb.at += 16 * T
        s_abs.append(nc.alloc_sbuf_tensor_at("sb_abs_b", [P, NB], F32, offset=sb.at - 16 * T))
        p_inv = sb.take("inv", [P, 4, 16])
        pool_w = nc.alloc_sbuf_tensor_at("pool_w", [P, 4, P], F32, offset=sb.at); sb.at += 16 * P
        s_mask_raw = nc.alloc_sbuf_tensor_at("sb_mask_raw", [P, P], F32, offset=sb.at); sb.at += 4 * P
        assert sb.at <= arena_end, sb.at - arena_end
        pw = [s_abs[0][:, 0:T], s_sum[:, 0:T]]
        ORDER = (3, 1, 2, 0)
        SCORED = {3: 1, 1: 2, 2: 4, 0: 4}
        GROUPS = ((slice(6 * P, NB), (3,)), (slice(0, 6 * P), (1, 2, 0)))

        def pe_sb(pe):
            pe_tokens(pe, 4, "sb_v", 32)
            pe.wait_ge(sem("tokens_out"), 40)
            for i in range(4):
                pe_unit(pe, 4, i, u_of("sb_x") + i, i)
            wait(pe, "sb_px", 4)
            u0 = u_of("sb_qk")
            for c in range(2):
                pe_unit(pe, 4, c, u0 + c, c)
            pe.wait_ge(sem("sb_consts"), 16 * 4)
            for i in range(4):
                wait(pe, "sb_pooled", i + 1)
                nc.tensor.matmul(ps[4 + i][:], pool_w[:, i, :], px[:, i, :], start=True, stop=True).then_inc(sem("sb_mixed"), 1)
            wait(pe, "sb_pool_out", 4)
            qh, ql_, kh, kl_ = sq_hi, sq_lo, sk_hi, sk_lo

            def scores(hd, head):
                for qt in ORDER:
                    n, at = P * (qt + 1), S_AT[qt]
                    sl = slice(qt * P, (qt + 1) * P)
                    out = ps[S_BANK[qt]][:, at:at + n]
                    wait(pe, "sb_left", 4 * (head - 1) + SCORED[qt])
                    mm3(out, [qh[hd][:, sl], ql_[hd][:, sl]], [kh[:, 0:n], kl_[:, 0:n]], True, False)
                    nc.tensor.matmul(out[:, n - P:n], s_ident[:], s_neg[:], start=False, stop=True).then_inc(sem("sb_scores"), 1)

            def values():
                for kt in range(TT):
                    n = T - kt * P
                    sl = slice(PT_AT[kt], PT_AT[kt] + n)
                    ins = mm3(ps[7][:, kt * P:T], [x[:, kt, :] for x in svs], [spt_hi[:, sl], spt_lo[:, sl]], kt == 0, kt == TT - 1)
                ins.then_inc(sem("sb_pv"), 1)

            def norm_sum(bank, square, n):
                wait(pe, "sb_square", n)
                nc.tensor.matmul(ps[bank][:], s_block[:], square, start=True, stop=True).then_inc(sem("sb_ms"), 1)

            def out_ready(e, k):
                if k < 4:
                    wait(e, "sb_out", 2 * (k + 1))

            def turn(head):
                wait(pe, "sb_prob", 2 * head + 2)
                wait(pe, "sb_out", head)
                transpose_pe(pe, s_prob).then_inc(sem("sb_turned"), 1)

            def bring(head):
                wait(pe, "sb_pt", head + 1)
                values()

            def step(p, par, do_proj, do_mix, last):
                m = p - 1
                before = do_mix and not (isinstance(m, int) and m == 0)
                if do_mix:
                    wait(pe, "sb_qk", m + 1)
                    scores(0, 2 * m)
                if before:
                    turn(2 * m - 1)
                first = isinstance(p, int) and p == 0
                if first:
                    pass
                elif do_proj:
                    pe_unit(pe, 4, 2 * par, u0 + 2 * p, 0)
                else:
                    out_early(pe, "sb_out", 0, [4, 5, 6, 7, 0, 1], out_ready)
                if before:
                    bring(2 * m - 1)
                if do_mix:
                    scores(1, 2 * m + 1)
                    turn(2 * m)
                if do_proj:
                    if not first:
                        pe_unit(pe, 4, 2 * par + 1, u0 + 2 * p + 1, 1)
                    norm_sum(0, B[0], 2 * p + 1)
                    norm_sum(1, B[1], 2 * p + 2)
                else:
                    out_early(pe, "sb_out", 1, [4, 5, 6, 7, 0, 1], out_ready)
                if do_mix:
                    wait(pe, "sb_vs", m + 1)
                    bring(2 * m)
                    if not do_proj:
                        out_early(pe, "sb_out", 0, [2], out_ready)
                        turn(2 * m + 1)
                        out_early(pe, "sb_out", 1, [2], out_ready)
                        bring(2 * m + 1)
            steps(pe, 4, step)
            pe_out(pe, 4, "sb_out", out_ready)

        def act_sb(act):
            act_tokens(act, "sb_v", lambda cb, tt: sv[:, 2 * cb:2 * cb + 2, tt, :], 32)
            for i in range(4):
                ahead(convert_act, act, "sb_x", i, u_of("sb_x") + i, True)
                used(act, u_of("sb_x") + i)
                nc.scalar.activation(px[:, i, :], ps[i][:], ACT.Copy).then_inc(sem("sb_px"), 1)
            for i in range(4):
                wait(act, "sb_mixed", i + 1)
                c = COL["pool_scale"] + i
                nc.scalar.activation(B[i % 2], ps[4 + i][:], ACT.Copy, scale=cols[:, c:c + 1]).then_inc(sem("sb_pscaled"), 1)
                wait(act, "sb_pscaled", i + 1)
                wait(act, "sb_pool_out", i)
                nc.scalar.activation(mix_hi[:, 4 + i, :], B[i % 2], ACT.Copy).then_inc(sem("sb_phi"), 1)
            u0 = u_of("sb_qk")

            def rstd_of(bank, n, out):
                wait(act, "sb_ms", n)
                nc.scalar.activation(out, ps[bank][:], ACT.Ln, bias=EPS, scale=1.0 / SB_DIM).then_inc(sem("sb_ln"), 1)
                wait(act, "sb_ln", n)
                nc.scalar.activation(out, out, ACT.Exp, scale=-0.5).then_inc(sem("sb_rstd"), 1)

            def front(head, buf):
                for n_, (sl, tiles) in enumerate(GROUPS):
                    wait(act, "sb_prob", 2 * head - 3 + n_)
                    for qt in tiles:
                        n = P * (qt + 1)
                        wait(act, "sb_scores", 4 * head + SCORED[qt])
                        ins = nc.scalar.activation(buf[:, PROB_AT[qt]:PROB_AT[qt] + n], ps[S_BANK[qt]][:, S_AT[qt]:S_AT[qt] + n],
                                                   ACT.Abs)
                    ins.then_inc(sem("sb_abs"), 1)
                    wait(act, "sb_abs", 2 * head + n_ + 1)
                    nc.scalar.activation(s_sum[:, sl], buf[:, sl], ACT.Exp, scale=-1.0).then_inc(sem("sb_e"), 1)
                    wait(act, "sb_e", 2 * head + n_ + 1)
                    nc.scalar.activation(buf[:, sl], s_sum[:, sl], ACT.Ln, bias=1.0).then_inc(sem("sb_l"), 1)

            def weights(head, buf):
                wait(act, "sb_turned", head)
                for n_, (sl, tiles) in enumerate(GROUPS):
                    wait(act, "sb_left", 4 * head + SCORED[tiles[-1]])
                    nc.scalar.activation(s_prob[:, sl], buf[:, sl], ACT.Exp).then_inc(sem("sb_prob"), 1)

            def turned(head):
                wait(act, "sb_turned", head + 1)
                wait(act, "sb_pv", head)
                for bank, at, n, to in PT_PARTS:
                    nc.scalar.activation(spt_hi[:, to:to + n], ps[bank][:, at:at + n], ACT.Copy).then_inc(sem("sb_pth"), 1)

            def output(head, hd, m):
                wait(act, "sb_pv", head + 1)
                r = ROWS[hd]
                nc.scalar.activation(mix_hi[r, m, :], ps[7][r, :], ACT.Copy).then_inc(sem("sb_outh"), 1)

            def project(p, n, raw_, bank):
                used(act, u0 + 2 * p + n)
                wait(act, "sb_qk", p)
                nc.scalar.activation(raw_[:], ps[bank][:], ACT.Copy)
                nc.scalar.activation(B[n], ps[bank][:], ACT.Square).then_inc(sem("sb_square"), 1)

            def step(p, par, do_proj, do_mix, last):
                m = p - 1
                before = do_mix and not (isinstance(m, int) and m == 0)
                if do_mix:
                    front(2 * m, s_abs[0])
                if do_proj:
                    ahead(convert_act, act, "sb_qk", 2 * par, u0 + 2 * p, last)
                if before:
                    turned(2 * m - 1)
                if do_mix:
                    weights(2 * m, s_abs[0])
                if do_proj:
                    project(p, 0, qraw, 0)
                if before:
                    output(2 * m - 1, 1, m - 1)
                if do_mix:
                    front(2 * m + 1, s_abs[1])
                    turned(2 * m)
                if do_proj:
                    ahead(convert_act, act, "sb_qk", 2 * par + 1, u0 + 2 * p + 1, last)
                    project(p, 1, kraw, 1)
                if do_mix:
                    weights(2 * m + 1, s_abs[1])
                if do_proj:
                    rstd_of(0, 2 * p + 1, B[3])
                    rstd_of(1, 2 * p + 2, B[4])
                    wait(act, "sb_qkn", 2 * p + 1)
                    if do_mix:
                        wait(act, "sb_scores", 8 * m + 8)
                    for hd in range(2):
                        nc.scalar.activation(sq_hi[hd][ROWS[hd], :], qraw[ROWS[hd], :], ACT.Copy, scale=0.125).then_inc(sem("sb_qh"), 1)
                    wait(act, "sb_qkn", 2 * p + 2)
                    nc.scalar.activation(sk_hi[:], kraw[:], ACT.Copy).then_inc(sem("sb_kh"), 1)
                if do_mix:
                    output(2 * m, 0, m)
                    if not do_proj:
                        turned(2 * m + 1)
                        output(2 * m + 1, 1, m)
            wait(act, "sb_pool_out", 4)
            steps(act, 4, step)
            act_out(act, 4, "sb_out")

        def dve_sb(dve):
            dve.wait_ge(sem("x_ready"), 8 * 4 + 8)
            for t in (sq_hi, sq_lo):
                nc.vector.memset(t[0][ROWS[1], :].bitcast(F32), 0.0)
                nc.vector.memset(t[1][ROWS[0], :].bitcast(F32), 0.0)
            nc.vector.memset(s_ones[:], 1.0).then_inc(sem("sb_ones"), 1)
            dve.wait_ge(sem("sb_consts"), 16 * 4)
            nc.vector.tensor_copy(s_neg[:], s_mask_raw[:])
            nc.vector.tensor_copy(s_ident[:], ident[:]).then_inc(sem("sb_ones"), 1)
            dve_ahead_only(dve, "sb_v")
            k = 0
            for i in range(4):
                ahead(convert_dve, dve, "sb_x", i, u_of("sb_x") + i, True)
                wait(dve, "sb_px", i + 1)
                src = px[:, i, :]
                for r in range(i + 1):
                    sh = 1 << r
                    wait(dve, "sb_window", k)
                    dst = pw[k % 2]
                    nc.vector.tensor_copy(dst[:, 0:sh], src[:, 0:sh])
                    nc.vector.tensor_tensor(dst[:, sh:T], src[:, sh:T], src[:, 0:T - sh], ALU.add).then_inc(sem("sb_window"), 1)
                    src = dst
                    k += 1
                wait(dve, "sb_window", k)
                dst = pw[k % 2]
                width = 2 << i
                nc.vector.tensor_tensor(dst[:, 0:16], src[:, 0:16], p_inv[:, i, :], ALU.mult)
                nc.vector.tensor_scalar(dst[:, 16:T], src[:, 16:T], 1.0 / width, None, ALU.mult).then_inc(sem("sb_window"), 1)
                k += 1
                wait(dve, "sb_window", k)
                nc.vector.tensor_tensor(px[:, i, :], dst, px[:, i, :], ALU.subtract).then_inc(sem("sb_pooled"), 1)
            for i in range(4):
                wait(dve, "sb_phi", i + 1)
                nc.vector.tensor_tensor(mix_lo[:, 4 + i, :], B[i % 2], mix_hi[:, 4 + i, :].bitcast(F32),
                                        ALU.subtract).then_inc(sem("sb_pool_out"), 1)
            u0 = u_of("sb_qk")

            def remaining(head, buf):
                done = 0
                for n_, (_, tiles) in enumerate(GROUPS):
                    wait(dve, "sb_l", 2 * head + n_ + 1)
                    for qt in tiles:
                        n = P * (qt + 1)
                        sl = slice(PROB_AT[qt], PROB_AT[qt] + n)
                        z = ps[S_BANK[qt]][:, S_AT[qt]:S_AT[qt] + n]
                        nc.vector.scalar_tensor_tensor(s_sum[:, sl], z, 0.0, buf[:, sl], ALU.max, ALU.add).then_inc(sem("sb_sp"), 1)
                    for k_, qt in enumerate(tiles):
                        n = P * (qt + 1)
                        a = PROB_AT[qt]
                        wait(dve, "sb_sp", 4 * head + done + k_ + 1)
                        rev = s_sum[:, a:a + n][:, ::-1]
                        nc.vector.tensor_tensor_scan(rev, s_ones[:, 0:n], rev, 0.0, ALU.mult, ALU.add).then_inc(sem("sb_cum"), 1)
                    for k_, qt in enumerate(tiles):
                        n = P * (qt + 1)
                        sl = slice(PROB_AT[qt], PROB_AT[qt] + n)
                        z = ps[S_BANK[qt]][:, S_AT[qt]:S_AT[qt] + n]
                        wait(dve, "sb_cum", 4 * head + done + k_ + 1)
                        nc.vector.tensor_tensor(buf[:, sl], z, s_sum[:, sl], ALU.subtract).then_inc(sem("sb_left"), 1)
                    done += len(tiles)

            def turned(head):
                for n_, (bank, at, n, to) in enumerate(PT_PARTS):
                    wait(dve, "sb_pth", 3 * head + n_ + 1)
                    ins = nc.vector.tensor_tensor(spt_lo[:, to:to + n], ps[bank][:, at:at + n],
                                                  spt_hi[:, to:to + n].bitcast(F32), ALU.subtract)
                ins.then_inc(sem("sb_pt"), 1)

            def output(head, hd, m):
                wait(dve, "sb_outh", head + 1)
                r = ROWS[hd]
                nc.vector.tensor_tensor(mix_lo[r, m, :], ps[7][r, :], mix_hi[r, m, :].bitcast(F32),
                                        ALU.subtract).then_inc(sem("sb_out"), 1)

            def step(p, par, do_proj, do_mix, last):
                m = p - 1
                before = do_mix and not (isinstance(m, int) and m == 0)
                if do_mix:
                    remaining(2 * m, s_abs[0])
                if do_proj:
                    ahead(convert_dve, dve, "sb_qk", 2 * par, u0 + 2 * p, last)
                if before:
                    turned(2 * m - 1)
                    output(2 * m - 1, 1, m - 1)
                if do_mix:
                    remaining(2 * m + 1, s_abs[1])
                    turned(2 * m)
                if do_proj:
                    ahead(convert_dve, dve, "sb_qk", 2 * par + 1, u0 + 2 * p + 1, last)
                if do_proj:
                    wait(dve, "sb_rstd", 2 * p + 1)
                    nc.vector.scalar_tensor_tensor(qraw[:], qraw[:], cols[:, COL["sb_q"]:COL["sb_q"] + 1], B[3], ALU.mult,
                                                   ALU.mult).then_inc(sem("sb_qkn"), 1)
                    wait(dve, "sb_rstd", 2 * p + 2)
                    nc.vector.scalar_tensor_tensor(kraw[:], kraw[:], cols[:, COL["sb_k"]:COL["sb_k"] + 1], B[4], ALU.mult,
                                                   ALU.mult).then_inc(sem("sb_qkn"), 1)
                    wait(dve, "sb_qkn", 2 * p + 2)
                    for hd in range(2):
                        r = ROWS[hd]
                        wait(dve, "sb_qh", 2 * p + hd + 1)
                        nc.vector.scalar_tensor_tensor(sq_lo[hd][r, :], qraw[r, :], 0.125, sq_hi[hd][r, :].bitcast(F32),
                                                       ALU.mult, ALU.subtract)
                    wait(dve, "sb_kh", p + 1)
                    nc.vector.tensor_tensor(sk_lo[:], kraw[:], sk_hi[:].bitcast(F32), ALU.subtract).then_inc(sem("sb_qk"), 1)
                if do_mix:
                    output(2 * m, 0, m)
                    if not do_proj:
                        turned(2 * m + 1)
                        output(2 * m + 1, 1, m)
            steps(dve, 4, step)
            dve_out(dve, 4, "sb_out")

        def pool_sb(pool):
            pool.wait_ge(sem("x_ready"), 8 * 4 + 1)
            for dst, name in ((s_mask_raw, "negmask_strict"), (s_block, "block_ones"), (p_inv, "pool_inv"), (pool_w, "pool_w")):
                nc.gpsimd.dma_start(dst[:], io[name]).then_inc(sem("sb_consts"), 16)
            stage_values(pool, sv, svs, 4, "sb", 40, "sb_pv", 2)

        ga, ga_v, ga_g = mixer_region("gla")
        gv = ga_v[:].rearrange("p (m t c) -> p m t c", m=4, t=TT)
        ggate = ga_g[:].rearrange("p (m t) -> p m t", m=8)
        gmix_at = 8 * T
        gq = ga.take("q", [P, T])
        gqs = [ga.take(f"q_{x}", [P, T], F32R) for x in ("hi", "lo")]
        gcum = ga.take("cum", [P, 4, T])
        gkd = [ga.take(f"kd_{x}", [P, 2, TT, P], F32R) for x in ("hi", "lo")]
        gvs = [ga.take(f"vs_{x}", [P, TT, 2 * P], F32R) for x in ("hi", "lo")]
        at_st = ga.at
        gst = ga.take("st", [P, NCH, 2 * P])
        gsts = [ga.take(f"st_{x}", [P, NCH, 2 * P], F32R) for x in ("hi", "lo")]
        gdec = ga.take("dec", [P, NCH])
        G = Region("gla_setup"); G.at = at_st
        g_raw = G.take("raw", [P, IN_UNIT])
        g_hi = G.take("hi", [P, IN_UNIT], F32R)
        g_lo = G.take("lo", [P, IN_UNIT], F32R)
        a_low = G.take("a_low", [P, T])
        w_a2 = G.take("w_a2", [16, T])
        g_scan = G.take("scan_mask", [P, T])
        assert G.at <= at_st + 24 * 1024
        g_ls = nc.alloc_sbuf_tensor_at("gla_ls", [P, 4, T], F32, offset=at_st - 8 * 1024)

        def gla_steps(step):
            step(0, 0, True, False, False, False)
            step(1, 1, True, True, False, False)
            step(2, 0, True, True, True, False)
            step(3, 1, True, True, True, True)
            step(4, 0, False, True, True, True)
            step(5, 1, False, False, True, True)

        def pe_gla(pe):
            pe_tokens(pe, 6, "gla_v", 40)
            wait(pe, "gla_gate", 1)
            for k in range(DT):
                ins = mm3(ps[4][:], [x[:, k * P:(k + 1) * P] for x in (g_hi, g_lo)], [x_hi[:, k, :], x_lo[:, k, :]],
                          k == 0, k == DT - 1)
            ins.then_inc(sem("gla_low"), 1)
            wait(pe, "gla_alow", 1)
            wait(pe, "gla_consts", 16 * 3)
            for i in range(4):
                ins = nc.tensor.matmul(ps[4 + i][:], w_a2[:, i * P:(i + 1) * P], a_low[0:16, :], start=True, stop=True)
                ins.then_inc(sem("gla_logit"), 1)
            pe.wait_ge(sem("tokens_out"), 56)
            pe_gates(pe, 6, "gla_r", 8)
            pe.wait_ge(sem("gates_out"), 16)
            wait(pe, "gla_min", 4)
            u0 = u_of("gla_qk")

            def out_ready(e, k):
                wait(e, "gla_out", k + 1)

            def step(p, par, do_proj, do_mix, do_norm, last):
                m, o = p - 1, p - 2
                if do_mix:
                    wait(pe, "gla_kd", m + 1)
                    wait(pe, "gla_st", 8 * m)
                    pe_turn_kd(pe, 6, B[1]).then_inc(sem("gla_kdt"), 1)
                if do_proj:
                    wait(pe, "gla_q", p)
                    pe.wait_ge(sem("split_ready"), u0 + 2 * p + 1)
                    pe_unit_k(2 * par, 0, range(4))
                if do_mix:
                    wait(pe, "gla_kds", m + 1)
                    wait(pe, "gla_vs", m + 1)
                    for c in range(NCH):
                        out = ps[3 + c // 2][:, (c % 2) * 256:(c % 2 + 1) * 256]
                        ins = mm3(out, [x[:, c % 2, c // 2, :] for x in gkd], [x[:, c // 2, :] for x in gvs], True, True)
                        if c % 2:
                            ins.then_inc(sem("gla_ds"), 1)
                if p == 5:
                    out_early(pe, "gla_out", 0, [4], out_ready)
                if do_norm:
                    wait(pe, "gla_sqs", o + 1)
                    nc.tensor.matmul(ps[1][:], ones[:], B[2], start=True, stop=True).then_inc(sem("gla_ms"), 1)
                if do_proj:
                    pe_unit_k(2 * par, 0, range(4, DT))
                    wait(pe, "gla_kd", p)
                    wait(pe, "gla_rstd", 2 * o + 1)
                    pe.wait_ge(sem("split_ready"), u0 + 2 * p + 2)
                    pe_unit_k(2 * par + 1, 1, range(4))
                if p == 4:
                    wait(pe, "gla_q", 4)
                    out_early(pe, "gla_out", 0, [0, 1, 2, 3], out_ready)
                if p == 5:
                    wait(pe, "gla_rstd", 7)
                    out_early(pe, "gla_out", 1, [0, 1, 2, 3, 4, 5], out_ready)
                    out_early(pe, "gla_out", 0, [5], out_ready)
                if do_mix:
                    wait(pe, "gla_qs", m + 1)
                    wait(pe, "gla_on", 2 * m)
                for c in range(NCH):
                    if do_proj and c % 2 == 0:
                        pe_unit_k(2 * par + 1, 1, [4 + c // 2])
                    if do_mix:
                        if c % 4 == 0:
                            wait(pe, "gla_sts", 2 * m + c // 4 + 1)
                        for vt in range(2):
                            sl = slice(c * CHUNK, (c + 1) * CHUNK)
                            ins = mm3(ps[7 if vt == 0 else 2][:, sl], [x[:, c, vt * P:(vt + 1) * P] for x in gsts],
                                      [x[:, sl] for x in gqs], True, True)
                if do_mix:
                    ins.then_inc(sem("gla_o"), 1)
            gla_steps(step)
            pe_out(pe, 6, "gla_out", out_ready)

        def act_gla(act):
            wait(act, "gla_consts", 16 * 3)
            nc.scalar.activation(g_hi[:], g_raw[:], ACT.Copy).then_inc(sem("gla_gate_hi"), 1)
            act_tokens(act, "gla_v", lambda cb, tt: gv[:, cb, tt, :], 40)
            wait(act, "gla_low", 1)
            nc.scalar.activation(a_low[:], ps[4][:], ACT.Copy).then_inc(sem("gla_alow"), 1)
            for i in range(4):
                wait(act, "gla_logit", i + 1)
                c = COL["gla_b"] + i
                nc.scalar.activation(g_ls[:, i, :], ps[4 + i][:], ACT.Abs, bias=cols[:, c:c + 1]).then_inc(sem("gla_abs"), 1)
            wait(act, "gla_abs", 4)
            nc.scalar.activation(g_ls[:], g_ls[:], ACT.Exp, scale=-1.0).then_inc(sem("gla_exp"), 1)
            wait(act, "gla_exp", 1)
            nc.scalar.activation(g_ls[:], g_ls[:], ACT.Ln, bias=1.0).then_inc(sem("gla_ln"), 1)
            act_gates(act, "gla_r", ggate)
            u0 = u_of("gla_qk")

            def step(p, par, do_proj, do_mix, do_norm, last):
                m, o = p - 1, p - 2
                if do_norm:
                    wait(act, "gla_o", o + 1)
                    wait(act, "gla_out", 2 * o)
                    for vt in range(2):
                        nc.scalar.activation(B[vt + 2], ps[7 if vt == 0 else 2][:], ACT.Square).then_inc(sem("gla_sq"), 1)
                if do_mix:
                    wait(act, "gla_kdt", m + 1)
                    wait(act, "gla_ds", 4 * m)
                    for half in range(2):
                        nc.scalar.activation(gkd[0][ROWS[half], half, :, :], ps[6][ROWS[half], :].rearrange("p (t c) -> p t c", t=TT),
                                             ACT.Copy).then_inc(sem("gla_kdh"), 1)
                    wait(act, "gla_o", m)
                    nc.scalar.activation(gqs[0][:], gq[:], ACT.Copy).then_inc(sem("gla_qh"), 1)
                if do_proj:
                    ahead(convert_act, act, "gla_qk", 2 * par, u0 + 2 * p, last)
                if do_norm:
                    wait(act, "gla_ms", o + 1)
                    nc.scalar.activation(B[3], ps[1][:], ACT.Ln, bias=EPS, scale=1.0 / 256).then_inc(sem("gla_rstd"), 1)
                    wait(act, "gla_rstd", 2 * o + 1)
                    nc.scalar.activation(B[4], B[3], ACT.Exp, scale=-0.5).then_inc(sem("gla_rstd"), 1)
                if do_mix:
                    for half in range(2):
                        wait(act, "gla_st", 8 * m + 4 * half + 4)
                        sl = slice(4 * half, 4 * half + 4)
                        nc.scalar.activation(gsts[0][:, sl, :], gst[:, sl, :], ACT.Copy).then_inc(sem("gla_sth"), 1)
                if do_norm:
                    for vt in range(2):
                        wait(act, "gla_og", 2 * o + vt + 1)
                        nc.scalar.activation(mix_hi[:, 2 * o + vt, :], B[2 + vt], ACT.Copy).then_inc(sem("gla_outh"), 1)
                if do_proj:
                    ahead(convert_act, act, "gla_qk", 2 * par + 1, u0 + 2 * p + 1, last)
                    used(act, u0 + 2 * p)
                    wait(act, "gla_qs", p)
                    nc.scalar.activation(gq[:], ps[0][:], ACT.Copy, scale=float(P) ** -0.5).then_inc(sem("gla_q"), 1)
                    wait(act, "gla_diff", p + 1)
                    nc.scalar.activation(B[0], B[1], ACT.Exp, scale=1.0 / GLA_TAU).then_inc(sem("gla_decay"), 1)
                    wait(act, "gla_st", 8 * p)
                    nc.scalar.activation(gdec[:], gcum[:, bass.ds(p, 1), :].rearrange("p a (g x) -> p (a g) x", x=CHUNK)[:, :, CHUNK - 1],
                                         ACT.Exp, scale=1.0 / GLA_TAU).then_inc(sem("gla_dec"), 1)
            gla_steps(step)
            act_out(act, 6, "gla_out")

        def dve_gla(dve):
            dve.wait_ge(sem("x_ready"), 8 * 6 + 8)
            for t in gkd:
                nc.vector.memset(t[ROWS[1], 0, :, :].bitcast(F32), 0.0)
                nc.vector.memset(t[ROWS[0], 1, :, :].bitcast(F32), 0.0)
            wait(dve, "gla_gate_hi", 1)
            nc.vector.tensor_tensor(g_lo[:], g_raw[:], g_hi[:].bitcast(F32), ALU.subtract).then_inc(sem("gla_gate"), 1)
            dve_ahead_only(dve, "gla_v")
            for i in range(4):
                wait(dve, "gla_abs", i + 1)
                c = COL["gla_b"] + i
                nc.vector.tensor_scalar(gcum[:, i, :], ps[4 + i][:], cols[:, c:c + 1], 0.0, ALU.add, ALU.min).then_inc(sem("gla_min"), 1)
            wait(dve, "gla_min", 4)
            wait(dve, "gla_ln", 1)
            for i in range(4):
                nc.vector.tensor_tensor(g_ls[:, i, :], gcum[:, i, :], g_ls[:, i, :], ALU.subtract).then_inc(sem("gla_la"), 1)
            for i in range(4):
                wait(dve, "gla_la", i + 1)
                nc.vector.tensor_tensor_scan(gcum[:, i, :], g_scan[:], g_ls[:, i, :], 0.0, ALU.mult, ALU.add).then_inc(sem("gla_cum"), 1)
            dve_ahead_only(dve, "gla_r")
            wait(dve, "gla_cum", 4)
            u0 = u_of("gla_qk")

            def step(p, par, do_proj, do_mix, do_norm, last):
                m, o = p - 1, p - 2
                if do_norm:
                    wait(dve, "gla_sq", 2 * o + 2)
                    nc.vector.tensor_tensor(B[2], B[2], B[3], ALU.add).then_inc(sem("gla_sqs"), 1)
                if do_mix:
                    for half in range(2):
                        wait(dve, "gla_kdh", 2 * m + half + 1)
                        r = ROWS[half]
                        ins = nc.vector.tensor_tensor(gkd[1][r, half, :, :], ps[6][r, :].rearrange("p (t c) -> p t c", t=TT),
                                                      gkd[0][r, half, :, :].bitcast(F32), ALU.subtract)
                    ins.then_inc(sem("gla_kds"), 1)
                    wait(dve, "gla_qh", m + 1)
                    nc.vector.tensor_tensor(gqs[1][:], gq[:], gqs[0][:].bitcast(F32), ALU.subtract).then_inc(sem("gla_qs"), 1)
                if do_proj:
                    ahead(convert_dve, dve, "gla_qk", 2 * par, u0 + 2 * p, last)
                if do_mix:
                    wait(dve, "gla_dec", m + 1)
                    for c in range(NCH):
                        wait(dve, "gla_ds", 4 * m + c // 2 + 1)
                        ds_ = ps[3 + c // 2][:, (c % 2) * 256:(c % 2 + 1) * 256]
                        if c == 0:
                            nc.vector.tensor_copy(gst[:, 0, :], ds_).then_inc(sem("gla_st"), 1)
                        else:
                            wait(dve, "gla_st", 8 * m + c)
                            nc.vector.scalar_tensor_tensor(gst[:, c, :], gst[:, c - 1, :], gdec[:, c:c + 1], ds_, ALU.mult,
                                                           ALU.add).then_inc(sem("gla_st"), 1)
                    for half in range(2):
                        wait(dve, "gla_sth", 2 * m + half + 1)
                        sl = slice(4 * half, 4 * half + 4)
                        nc.vector.tensor_tensor(gsts[1][:, sl, :], gst[:, sl, :], gsts[0][:, sl, :].bitcast(F32),
                                                ALU.subtract).then_inc(sem("gla_sts"), 1)
                if do_norm:
                    wait(dve, "gla_rstd", 2 * o + 2)
                    for vt in range(2):
                        g = COL["gla_norm"] + vt
                        nc.vector.scalar_tensor_tensor(B[2 + vt], ps[7 if vt == 0 else 2][:], cols[:, g:g + 1], B[4], ALU.mult,
                                                       ALU.mult).then_inc(sem("gla_on"), 1)
                    for vt in range(2):
                        wait(dve, "gla_on", 2 * o + vt + 1)
                        nc.vector.tensor_tensor(B[2 + vt], B[2 + vt], ggate[:, 2 * o + vt, :], ALU.mult).then_inc(sem("gla_og"), 1)
                if do_proj:
                    wait(dve, "gla_kdt", p)
                    v = lambda t: t.rearrange("p (g x) -> p g x", x=CHUNK)
                    cum = gcum[:, bass.ds(p, 1), :].rearrange("p a (g x) -> p (a g) x", x=CHUNK)
                    nc.vector.tensor_tensor(v(B[1]), cum[:, :, CHUNK - 1:CHUNK].to_broadcast([P, NCH, CHUNK]), cum,
                                            ALU.subtract).then_inc(sem("gla_diff"), 1)
                if do_norm:
                    for vt in range(2):
                        wait(dve, "gla_outh", 2 * o + vt + 1)
                        nc.vector.tensor_tensor(mix_lo[:, 2 * o + vt, :], B[2 + vt], mix_hi[:, 2 * o + vt, :].bitcast(F32),
                                                ALU.subtract).then_inc(sem("gla_out"), 1)
                if do_proj:
                    ahead(convert_dve, dve, "gla_qk", 2 * par + 1, u0 + 2 * p + 1, last)
                    wait(dve, "gla_decay", p + 1)
                    used(dve, u0 + 2 * p + 1)
                    nc.vector.tensor_tensor(B[1], ps[1][:], B[0], ALU.mult).then_inc(sem("gla_kd"), 1)
            gla_steps(step)
            wait(dve, "gla_out", 8)
            dve_out(dve, 6, "gla_out")

        def pool_gla(pool):
            pool.wait_ge(sem("x_ready"), 8 * 6 + 1)
            for dst, name in ((g_raw, "gla_gate"), (w_a2, "w_a2"), (g_scan, "scan_mask")):
                nc.gpsimd.dma_start(dst[:], io[name]).then_inc(sem("gla_consts"), 16)
            wait(pool, "gla_cum", 4)
            stage_values(pool, gv, gvs, 4, "gla", 56, "gla_ds", 4)

        CONST_DMAS = 16 * 4
        SUB = {0: (pe_fox, act_fox, dve_fox, pool_fox), 2: (pe_hgrn, act_hgrn, dve_hgrn, pool_hgrn),
               4: (pe_sb, act_sb, dve_sb, pool_sb), 6: (pe_gla, act_gla, dve_gla, pool_gla)}
        block = ctx.enter_context(nc.Block())

        @block.sync
        def _(sp):
            sp.dma_start(cols[:], io["cols"]).then_inc(sem("consts_loaded"), 16)
            sp.dma_start(ident[:], io["ident"]).then_inc(sem("consts_loaded"), 16)
            sp.dma_start(ones[:], io["ones"]).then_inc(sem("consts_loaded"), 16)
            sp.dma_start(mask_raw[:], io["negmask"]).then_inc(sem("consts_loaded"), 16)
            for i in range(DT):
                sp.dma_start(h[:, i, :], io["x"][i]).then_inc(sem(f"h_loaded{i}"), 16)
            for name in order:
                ph = phases[name]
                u0 = ph.first
                src = io["w_" + name]
                if name == "fox_v":
                    for c in range(2):
                        sp.dma_start(raw[:, c, 0:ph.size], src[c]).then_inc(sem(f"raw_ready{c}"), 16)
                    sp.dma_start(gate_raw[:], io["fox_gate"]).then_inc(sem("gate_loaded"), 16)

                def load(i, c):
                    sp.wait_ge(sem("split_ready"), u0 + i - 1)
                    sp.dma_start(raw[:, c, 0:ph.size], src[i]).then_inc(sem(f"raw_ready{c}"), 16)
                first = 1 if name == "fox_v" else 0

                def body(j):
                    load(2 * j, 0)
                    load(2 * j + 1, 1)
                repeat(sp, first, ph.count // 2, body)
            for i in range(DT):
                sp.wait_ge(sem("h_ready"), 8 * (stop - 1) + i + 1)
                sp.dma_start(io["out"][i], h[:, i, :]).then_inc(sem("out_stored"), 16)
            sp.wait_ge(sem("out_stored"), 16 * DT)

        @block.tensor
        def _(pe):
            pe.sem_inc(sem("unit_used"), CREDIT)
            for name in CREDITED:
                pe.sem_inc(sem(name), 1)
            pe.wait_ge(sem("consts_loaded"), CONST_DMAS)
            pe_sum(pe, 0)
            for s in range(stop):
                SUB[s][0](pe) if s in SUB else pe_ffn(pe, s)

        @block.scalar
        def _(act):
            exp_ln_table()
            act.wait_ge(sem("consts_loaded"), CONST_DMAS)
            for i in range(DT):
                act.wait_ge(sem(f"h_loaded{i}"), 16)
                act_square(act, 0, i, i % 2, h[:, i, :])
                if i in (6, 7):
                    convert_act(act, i - 6, i - 6, IN_UNIT)
            act_rstd(act, 0)
            norm_act(act, 0)
            for s in range(stop):
                SUB[s][1](act) if s in SUB else act_ffn(act, s)

        @block.vector
        def _(dve):
            dve.sem_inc(sem("gated_ready"), 2)
            dve_sum_start(dve, 0)
            dve.wait_ge(sem("consts_loaded"), CONST_DMAS)
            for i in range(DT):
                dve_square(dve, 0, i, i % 2)
                if i in (6, 7):
                    convert_dve(dve, i - 6, i - 6, IN_UNIT)
            norm_dve(dve, 0)
            for s in range(stop):
                SUB[s][2](dve) if s in SUB else dve_ffn(dve, s)

        @block.gpsimd
        def _(pool):
            for s in range(stop):
                if s in SUB:
                    SUB[s][3](pool)


def _units(w, n):
    return w.reshape(DT, P, n, P).transpose(2, 1, 0, 3).reshape(n, P, IN_UNIT)


def _token_units(w):
    n = w.shape[1] // 256
    return w.reshape(2, 4, P, n, 256).transpose(3, 0, 2, 1, 4).reshape(2 * n, P, IN_UNIT)


def _down_units(w):
    return w.reshape(2, DOWN_BLOCKS, P, DT, P).transpose(3, 0, 2, 1, 4).reshape(2 * DT, P, DOWN_UNIT)


def _alternate(*parts):
    return np.stack(parts, 1).reshape(-1, *parts[0].shape[1:])


def _gate_unit(w, starts):
    wide = np.zeros((D, P), w.dtype)
    for a in starts:
        wide[:, a:a + w.shape[1]] = w
    return _units(wide, 1)[0]


def _level_masks():
    k, q = np.arange(P)[:, None], np.arange(P)[None, :]
    m = [(k // g == q // g) & (k % g < g // 2) & (q % g >= g // 2) for g in (64, 32, 16)]
    m.append((k // 8 == q // 8) & (k <= q))
    return np.stack(m, 1).astype(np.uint32)


def _cols(i):
    f = lambda a: a.reshape(-1, P).T
    c = np.zeros((P, N_COLS), np.float32)

    def put(name, a):
        c[:, COL[name]:COL[name] + a.shape[1]] = a
    put("gain", f(i["norm_gains"]))
    put("mix_even", f(i["mix_norm_even_2"]))
    put("ffn_norm0", f(i["ffn_norm_2"][0]))
    put("mix_odd", f(i["mix_norm_odd_2"]))
    put("ffn_norm1", f(i["ffn_norm_2"][1]))
    for a in range(0, P, 32):
        c[a:a + FOX_HEADS, COL["fox_b"]] = i["fox_b_f"][0]
        c[a:a + FOX_HEADS, COL["onehot"]:COL["onehot"] + FOX_HEADS] = np.eye(FOX_HEADS)
    put("lb_table", f(i["hgrn_lb_table"]))
    put("hgrn_norm", f(i["hgrn_gnorm"]))
    put("sb_q", f(np.concatenate([i["sb_q_gain_2"][0]] * 2)))
    put("sb_k", f(np.concatenate([i["sb_k_gain_2"][0]] * 2)))
    put("pool_scale", f(i["pool_scale_2"]))
    put("gla_b", f(i["gla_b_a_2"]))
    put("gla_norm", f(i["gla_o_gain_2"]))
    for l in range(2):
        taps = [_alternate(*np.split(a.reshape(-1, P), 2)).T for a in (*i["ffn_conv_w_2"][l], i["ffn_conv_b_2"][l])]
        put(f"conv{l}", np.concatenate(taps, 1))
    return c


def layout(i):
    i = {k: np.asarray(v) for k, v in i.items()}
    s = lambda w, a, n: w[:, a:a + n]
    fi, hi, ev, od = i["fox_w_in"][0], i["hgrn_w_in"][0], i["w_in_even_2"][0], i["w_in_odd_2"][0]
    a = {
        "x": i["x"][0].T.reshape(DT, P, T),
        "cols": _cols(i),
        "ident": np.eye(P, dtype=np.float32),
        "ones": np.ones((P, P), np.float32),
        "negmask": np.where(np.arange(P)[:, None] >= np.arange(P)[None, :], 0.0, NEG).astype(np.float32),
        "negmask_strict": np.where(np.arange(P)[:, None] > np.arange(P)[None, :], 0.0, NEG).astype(np.float32),
        "block_ones": np.kron(np.eye(2), np.ones((64, 64))).astype(np.float32),
        "pool_inv": np.tile((1.0 / np.minimum(np.arange(1, 17)[None, :], 2.0 ** np.arange(1, 5)[:, None])).astype(np.float32), (P, 1, 1)),
        "pool_w": i["pool_w_2"][0].transpose(1, 0, 2),
        "w_a2": i["gla_w_a2_2"][0],
        "lv_mask": _level_masks(),
        "scan_mask": np.tile((np.arange(T) % CHUNK != 0).astype(np.float32), (P, 1)),
        "fox_gate": _gate_unit(s(fi, 3 * D, FOX_HEADS), range(0, P, 32)),
        "w_fox_v": _token_units(s(fi, 2 * D, D)),
        "w_fox_qk": _alternate(_units(s(fi, 0, D), 8), _units(s(fi, D, D), 8)),
        "w_fox_out": _units(i["fox_w_out"][0], 8),
        "w_hgrn_v": _token_units(s(hi, 2 * D, D)),
        "w_hgrn_g": _units(s(hi, 3 * D, D), 8),
        "w_hgrn_qf": _alternate(_units(s(hi, 0, D), 8), _units(s(hi, D, D), 8)),
        "w_hgrn_out": _units(i["hgrn_w_out"][0], 8),
        "w_sb_v": _token_units(s(ev, 1024, 512)),
        "w_sb_x": _units(s(ev, 1536, 512), 4),
        "w_sb_qk": _alternate(_units(s(ev, 0, 512), 4), _units(s(ev, 512, 512), 4)),
        "w_sb_out": _units(i["w_out_even_2"][0], 8),
        "w_gla_v": _token_units(s(od, 1024, 1024)),
        "w_gla_r": _units(s(od, 2048, 1024), 8),
        "w_gla_qk": _alternate(_units(s(od, 0, 512), 4), _units(s(od, 512, 512), 4)),
        "gla_gate": _gate_unit(s(od, 3072, 16), [0]),
        "w_gla_out": _units(i["w_out_odd_2"][0], 8),
    }
    for f, (w_in, w_out) in enumerate([(i["ffn_w_in"][0], i["ffn_w_out"][0]), (i["ffn_w_in"][1], i["ffn_w_out"][1]),
                                       (i["ffn_w_up_2"][0], i["ffn_w_down_2"][0]), (i["ffn_w_up_2"][1], i["ffn_w_down_2"][1])]):
        a[f"w_up{f}"] = _alternate(_units(s(w_in, 0, FF), FT), _units(s(w_in, FF, FF), FT))
        a[f"w_down{f}"] = _down_units(w_out)
    return {k: np.ascontiguousarray(v) for k, v in a.items()}


def program(nc, arrays, stop=8):
    io = {n: nc.dram_tensor(f"in_{n}", a.shape, mybir.dt.from_np(a.dtype), kind="ExternalInput").ap()
          for n, a in arrays.items()}
    io["out"] = nc.dram_tensor("out_h", (DT, P, T), F32, kind="ExternalOutput").ap()
    build(nc, io, stop)


def kernel(**inputs):
    from concourse.bacc import Bacc
    from concourse.bass_utils import run_bass_kernel_spmd

    arrays = layout(inputs)
    nc = Bacc("TRN2", target_bir_lowering=False, num_devices=1)
    program(nc, arrays)
    r = run_bass_kernel_spmd(nc, [{f"in_{n}": a for n, a in arrays.items()}], core_ids=[0])
    return r.results[0]["out_h"].reshape(D, T).T.reshape(1, T, D)
```
